# Optimizing a Trainium2 kernel written in Bass

```python
import jax, jax.numpy as jnp
from jax import lax
import numpy as np

D_MODEL = 1024
BATCH = 1
SEQ = 256
DEPTH = 1

N_META = 16
CONV_DIM = 512
CONV_WIDTH = 31
N_HEADS = 8
QK_NOPE_DIM = 64
QK_ROPE_DIM = 32
QK_HEAD_DIM = QK_NOPE_DIM + QK_ROPE_DIM
V_HEAD_DIM = 64
Q_LORA_RANK = 256
KV_LORA_RANK = 128
ROPE_THETA = 10000.0
Q_BLOCK = 128
N_BRANCHES = 2
N_EXPERTS = 32
TOP_K = 4
D_FF = 1024
SWIGLU_LIMIT = 7.0
SWIGLU_ALPHA = 1.702
MOE_BLOCK = 256
NORM_EPS = 1e-6
NEG_INF = -1e30

COLS_CONV = 2 * CONV_DIM
COLS_Q = Q_LORA_RANK
COLS_KV = KV_LORA_RANK + QK_ROPE_DIM
COLS_GATE = N_BRANCHES * D_MODEL
IN_COLS = COLS_CONV + COLS_Q + COLS_KV + COLS_GATE
SPLITS = (COLS_CONV, COLS_CONV + COLS_Q, COLS_CONV + COLS_Q + COLS_KV)

kernel_name = 'hybrid_meta_conv_mla_moe_layer'

def rms_norm(x, w):
    xf = x.astype(jnp.float32)
    y = xf * lax.rsqrt(jnp.mean(xf * xf, axis=-1, keepdims=True) + NORM_EPS)
    return (y * w.astype(jnp.float32)).astype(x.dtype)

def layer_norm(x, w, b):
    xf = x.astype(jnp.float32)
    mu = jnp.mean(xf, axis=-1, keepdims=True)
    xc = xf - mu
    y = xc * lax.rsqrt(jnp.mean(xc * xc, axis=-1, keepdims=True) + NORM_EPS)
    return (y * w.astype(jnp.float32) + b.astype(jnp.float32)).astype(x.dtype)

def apply_rope(x, pos):
    half = QK_ROPE_DIM // 2
    inv_freq = ROPE_THETA ** (-jnp.arange(half, dtype=jnp.float32) / half)
    ang = pos.astype(jnp.float32)[:, None] * inv_freq[None, :]
    cos = jnp.cos(ang)[:, None, :]
    sin = jnp.sin(ang)[:, None, :]
    xf = x.astype(jnp.float32)
    x1, x2 = xf[..., :half], xf[..., half:]
    return jnp.concatenate([x1 * cos - x2 * sin, x2 * cos + x1 * sin], axis=-1).astype(x.dtype)

def conformer_conv(u, dw_w, dw_b, ln_w, ln_b, w_pw2):
    a, g = u[..., :CONV_DIM], u[..., CONV_DIM:]
    h = a * jax.nn.sigmoid(g)
    h = lax.conv_general_dilated(
        h, dw_w[:, None, :].astype(h.dtype), window_strides=(1,),
        padding=[(CONV_WIDTH - 1, 0)], dimension_numbers=('NWC', 'WIO', 'NWC'),
        feature_group_count=CONV_DIM) + dw_b
    h = jax.nn.silu(layer_norm(h, ln_w, ln_b))
    return h @ w_pw2

def _attend(qb, qpos, k, v):
    s = jnp.einsum('bhqd,bhkd->bhqk', qb, k).astype(jnp.float32) * (QK_HEAD_DIM ** -0.5)
    kpos = jnp.arange(k.shape[2])
    s = jnp.where(kpos[None, :] <= qpos[:, None], s, NEG_INF)
    p = jax.nn.softmax(s, axis=-1).astype(v.dtype)
    return jnp.einsum('bhqk,bhkd->bhqd', p, v)

def causal_block_attention(q, k, v):
    B, H, L, dh = q.shape
    n_real = L - N_META
    nb = n_real // Q_BLOCK
    o_meta = _attend(q[:, :, :N_META], jnp.arange(N_META), k[:, :, :N_META], v[:, :, :N_META])
    q_blocks = q[:, :, N_META:].reshape(B, H, nb, Q_BLOCK, dh).transpose(2, 0, 1, 3, 4)
    pos_blocks = (N_META + jnp.arange(n_real)).reshape(nb, Q_BLOCK)
    o_real = lax.map(lambda a: _attend(a[0], a[1], k, v), (q_blocks, pos_blocks))
    o_real = o_real.transpose(1, 2, 0, 3, 4).reshape(B, H, n_real, V_HEAD_DIM)
    return jnp.concatenate([o_meta, o_real], axis=2)

def mla(q_lat, kv_lat, pos, q_a_norm_w, w_q_b, kv_a_norm_w, w_kv_b, q_norm_w, k_norm_w, w_o):
    B, L, _ = q_lat.shape
    q = (rms_norm(q_lat, q_a_norm_w) @ w_q_b).reshape(B, L, N_HEADS, QK_HEAD_DIM)
    c_kv, k_pe = kv_lat[..., :KV_LORA_RANK], kv_lat[..., KV_LORA_RANK:]
    kv = (rms_norm(c_kv, kv_a_norm_w) @ w_kv_b).reshape(B, L, N_HEADS, QK_NOPE_DIM + V_HEAD_DIM)
    k_nope, v = kv[..., :QK_NOPE_DIM], kv[..., QK_NOPE_DIM:]
    k_pe = jnp.broadcast_to(k_pe[:, :, None, :], (B, L, N_HEADS, QK_ROPE_DIM))
    k = jnp.concatenate([k_nope, k_pe], axis=-1)
    q = rms_norm(q, q_norm_w)
    k = rms_norm(k, k_norm_w)
    q = jnp.concatenate([q[..., :QK_NOPE_DIM], apply_rope(q[..., QK_NOPE_DIM:], pos)], axis=-1)
    k = jnp.concatenate([k[..., :QK_NOPE_DIM], apply_rope(k[..., QK_NOPE_DIM:], pos)], axis=-1)
    o = causal_block_attention(q.transpose(0, 2, 1, 3), k.transpose(0, 2, 1, 3), v.transpose(0, 2, 1, 3))
    o = o.transpose(0, 2, 1, 3).reshape(B, L, N_HEADS * V_HEAD_DIM)
    return o @ w_o

def moe(h, router_w, router_b, w_gate_up, b_gate_up, w_down, b_down):
    B, L, D = h.shape
    xt = h.reshape(-1, D)
    N = xt.shape[0]
    S = N * TOP_K
    logits = (xt @ router_w + router_b).astype(jnp.float32)
    top_val, top_idx = lax.top_k(logits, TOP_K)
    gates = jax.nn.softmax(top_val, axis=-1).astype(h.dtype)
    flat_e = top_idx.reshape(-1)
    order = jnp.argsort(flat_e)
    sorted_e = flat_e[order]
    counts = jnp.bincount(flat_e, length=N_EXPERTS)
    group_start = jnp.cumsum(counts) - counts
    padded = (counts + MOE_BLOCK - 1) // MOE_BLOCK * MOE_BLOCK
    padded_end = jnp.cumsum(padded)
    padded_start = padded_end - padded
    dest = (padded_start[sorted_e] + jnp.arange(S) - group_start[sorted_e]).astype(jnp.int32)
    n_blocks = S // MOE_BLOCK + N_EXPERTS + 1
    P = n_blocks * MOE_BLOCK
    row_token = jnp.zeros((P,), jnp.int32).at[dest].set((order // TOP_K).astype(jnp.int32))
    row_w = jnp.zeros((P,), h.dtype).at[dest].set(gates.reshape(-1)[order])
    block_expert = jnp.minimum(
        jnp.searchsorted(padded_end, jnp.arange(n_blocks) * MOE_BLOCK, side='right'), N_EXPERTS - 1)
    xs = xt[row_token].reshape(n_blocks, MOE_BLOCK, D)
    ws = row_w.reshape(n_blocks, MOE_BLOCK)

    def expert_block(args):
        xb, wb, e = args
        gu = xb @ w_gate_up[e] + b_gate_up[e]
        g, u = gu[:, :D_FF], gu[:, D_FF:]
        g = jnp.minimum(g, SWIGLU_LIMIT)
        u = jnp.clip(u, -SWIGLU_LIMIT, SWIGLU_LIMIT)
        act = (u + 1) * (g * jax.nn.sigmoid(SWIGLU_ALPHA * g))
        return (act @ w_down[e] + b_down[e]) * wb[:, None]

    ys = lax.map(expert_block, (xs, ws, block_expert)).reshape(P, D)
    y = jax.ops.segment_sum(ys, row_token, num_segments=N)
    return y.reshape(B, L, D)

def setup_inputs(seed: int = 0) -> dict:
    key = jax.random.key(seed)
    ks = jax.random.split(key, 32)
    f32 = jnp.float32

    def w(k, shape, fan_in):
        return jax.random.normal(k, shape, f32) * (fan_in ** -0.5)

    def gain(k, shape):
        return 1.0 + 0.02 * jax.random.normal(k, shape, f32)

    def bias(k, shape, s=0.02):
        return s * jax.random.normal(k, shape, f32)

    Dp = DEPTH
    return {
        'x': jax.random.normal(ks[0], (BATCH, SEQ, D_MODEL), f32),
        'meta_tokens': jax.random.normal(ks[1], (N_META, D_MODEL), f32),
        'attn_norm_w': gain(ks[2], (Dp, D_MODEL)),
        'w_in': w(ks[3], (Dp, D_MODEL, IN_COLS), D_MODEL),
        'conv_dw_w': w(ks[4], (Dp, CONV_WIDTH, CONV_DIM), CONV_WIDTH),
        'conv_dw_b': bias(ks[5], (Dp, CONV_DIM)),
        'conv_ln_w': gain(ks[6], (Dp, CONV_DIM)),
        'conv_ln_b': bias(ks[7], (Dp, CONV_DIM)),
        'conv_pw2_w': w(ks[8], (Dp, CONV_DIM, D_MODEL), CONV_DIM),
        'q_a_norm_w': gain(ks[9], (Dp, Q_LORA_RANK)),
        'w_q_b': w(ks[10], (Dp, Q_LORA_RANK, N_HEADS * QK_HEAD_DIM), Q_LORA_RANK),
        'kv_a_norm_w': gain(ks[11], (Dp, KV_LORA_RANK)),
        'w_kv_b': w(ks[12], (Dp, KV_LORA_RANK, N_HEADS * (QK_NOPE_DIM + V_HEAD_DIM)), KV_LORA_RANK),
        'q_norm_w': gain(ks[13], (Dp, QK_HEAD_DIM)),
        'k_norm_w': gain(ks[14], (Dp, QK_HEAD_DIM)),
        'w_o_mla': w(ks[15], (Dp, N_HEADS * V_HEAD_DIM, D_MODEL), N_HEADS * V_HEAD_DIM),
        'gate_b': bias(ks[16], (Dp, COLS_GATE)),
        'w_out': w(ks[17], (Dp, D_MODEL, D_MODEL), D_MODEL),
        'ffn_norm_w': gain(ks[18], (Dp, D_MODEL)),
        'router_w': w(ks[19], (Dp, D_MODEL, N_EXPERTS), D_MODEL),
        'router_b': bias(ks[20], (Dp, N_EXPERTS), 0.01),
        'w_gate_up': w(ks[21], (Dp, N_EXPERTS, D_MODEL, 2 * D_FF), D_MODEL),
        'b_gate_up': bias(ks[22], (Dp, N_EXPERTS, 2 * D_FF)),
        'w_down': w(ks[23], (Dp, N_EXPERTS, D_FF, D_MODEL), D_FF),
        'b_down': bias(ks[24], (Dp, N_EXPERTS, D_MODEL)),
    }

def reference(x, meta_tokens, attn_norm_w, w_in, conv_dw_w, conv_dw_b, conv_ln_w, conv_ln_b,
              conv_pw2_w, q_a_norm_w, w_q_b, kv_a_norm_w, w_kv_b, q_norm_w, k_norm_w, w_o_mla,
              gate_b, w_out, ffn_norm_w, router_w, router_b, w_gate_up, b_gate_up, w_down, b_down):
    B = x.shape[0]
    meta = jnp.broadcast_to(meta_tokens[None].astype(x.dtype), (B, N_META, D_MODEL))
    h = jnp.concatenate([meta, x], axis=1)
    L = h.shape[1]
    pos = jnp.arange(L)
    for l in range(DEPTH):
        hn = rms_norm(h, attn_norm_w[l])
        proj = hn @ w_in[l]
        u_conv, q_lat, kv_lat, g_lin = jnp.split(proj, SPLITS, axis=-1)
        y_conv = conformer_conv(u_conv, conv_dw_w[l], conv_dw_b[l], conv_ln_w[l], conv_ln_b[l], conv_pw2_w[l])
        y_mla = mla(q_lat, kv_lat, pos, q_a_norm_w[l], w_q_b[l], kv_a_norm_w[l], w_kv_b[l],
                    q_norm_w[l], k_norm_w[l], w_o_mla[l])
        g = jax.nn.sigmoid(g_lin + gate_b[l]).reshape(B, L, N_BRANCHES, D_MODEL)
        mixed = g[:, :, 0] * y_conv + g[:, :, 1] * y_mla
        h = h + mixed @ w_out[l]
        h = h + moe(rms_norm(h, ffn_norm_w[l]), router_w[l], router_b[l], w_gate_up[l], b_gate_up[l],
                    w_down[l], b_down[l])
    return h[:, N_META:]


_drawn_inputs = setup_inputs


def setup_inputs(seed=0):
    import zlib

    import numpy as np

    out = dict(_drawn_inputs(seed))
    spreads = {}
    factors = {'kv_a_norm_w': 3.008,
     'q_norm_w': 4.393,
     'k_norm_w': 3.296,
     'gate_b': 3.162,
     'b_gate_up': 5.309,
     'b_down': 6.093}
    for name, (base, spread) in spreads.items():
        noise = np.random.default_rng([zlib.crc32(name.encode()), seed]).standard_normal(out[name].shape)
        drawn = base * np.exp(spread * noise) if base else spread * noise
        out[name] = __import__('jax').numpy.asarray(drawn.astype(out[name].dtype))
    for name, factor in factors.items():
        out[name] = (out[name] * factor).astype(out[name].dtype)
    return out
```

```python
from contextlib import ExitStack

import numpy as np

import concourse.bass as bass
from concourse import mybir

F32 = mybir.dt.float32
BF16 = mybir.dt.bfloat16
I32 = mybir.dt.int32
U32 = mybir.dt.uint32
ALU = mybir.AluOpType
ACT = mybir.ActivationFunctionType
AX_X = mybir.AxisListType.X

P = 128
D = 1024
KD = D // P
SEQ = 256
META = 16
L = SEQ + META
CONV = 512
CT = CONV // P
TAPS = 31
PAD = TAPS - 1 - META
H = 8
NOPE, ROPE, VD = 64, 32, 64
HD = NOPE + ROPE
QL = 256
KVL = 128
COL_Q = 2 * CONV
COL_KV = COL_Q + QL
COL_G = COL_KV + KVL + ROPE
E = 32
TOPK = 4
FF = 1024
SLOTS = 64
EXTRA = SEQ * TOPK // SLOTS
LIMIT, ALPHA = 7.0, 1.702
EPS = 1e-6
NEG = -1e30
SCALE = float(HD) ** -0.5

C_ID, C_ONE, C_TRI, C_MASK, C_IOTA, C_RK, C_RQ, C_END = 0, 128, 256, 384, 656, 912, 1008, 1072
R_ATTN, R_DWB, R_LNW, R_LNB, R_QA, R_KVA, R_GB, R_END = 0, 8, 12, 16, 20, 22, 23, 39


def constants():
    c = np.zeros((P, C_END), np.float32)
    c[:, C_ID:C_ID + P] = np.eye(P)
    c[:, C_ONE:C_ONE + P] = 1.0
    c[:, C_TRI:C_TRI + P] = np.triu(np.ones((P, P)), 1)
    c[:, C_MASK + 144:C_MASK + 272] = np.triu(np.full((P, P), NEG), 1)
    c[:, C_IOTA:C_IOTA + 256] = np.arange(256)
    half = ROPE // 2
    inv = np.float32(10000.0) ** (-np.arange(half, dtype=np.float32) / np.float32(half))
    for col, first in [(C_RK, 0), (C_RK + 32, 128), (C_RK + 64, 256), (C_RQ, META), (C_RQ + 32, META + 128)]:
        ang = (first + np.arange(P)).astype(np.float32)[:, None] * inv[None, :].astype(np.float32)
        c[:, col:col + half] = np.cos(ang)
        c[:, col + half:col + 2 * half] = np.sin(ang)
    return c


def bank_plan():
    plan, turns = {}, [[] for _ in range(8)]

    def add(job, bank, release, value):
        plan[job] = (bank, len(turns[bank]), (release, value))
        turns[bank].append(job)

    add("par", 0, "par_ready", 1)
    for i, job in enumerate([("hn", 0, 0), ("hn", 0, 1), ("hn", 1, 0), ("hn", 1, 1), ("hn", 2, 0)]):
        add(job, 1 + i, "hn_ready", i + 1)
    order = [("ckv", "squares", 1), ("kpe", "kpe_ready", 1), ("q", "squares", 2)]
    conv = lambda j: [(("ca", j), "convin_ready", j + 1), (("cg", j), "csig_ready", j + 1)]
    order += conv(0) + [("ssk", "lvar_ready", 1), ("ssq", "lvar_ready", 2)] + conv(1)
    order += [(("kvb", t, c), "v_ready", 2 * t + c + 1) for t in range(3) for c in range(2)]
    order += [("kpet", "kraw_ready", 1)] + conv(2)
    order += [(("qb", t, c), "qraw_ready", 2 * t + c + 1) for t in range(2) for c in range(2)] + conv(3)
    order += [(("kt", t, c), "kT_ready", 2 * t + c + 1) for t in range(3) for c in range(2 if t < 2 else 1)]
    order += [(("qt", t, c), "qT_ready", 2 * t + c + 1) for t in range(2) for c in range(2)]
    for i, (job, release, value) in enumerate(order):
        add(job, (6 + i) % 8, release, value)
    for s in range(2 * H):
        add(("gate", s), 2 + s % 2, "gT_ready", s + 1)
        add(("s", s), 4 + s % 2, "max_ready", s + 1)
        add(("pt", s), 6 + s % 2, "probT_ready", s + 1)
        if s % 4 == 0:
            add(("ot", s // 4), s // 4 % 2, "oT_ready", s // 4 + 1)
    add("lnmu", 6, "lncent_ready", 1)
    add("lnvar", 7, "lnvar_ready", 1)
    for j in range(4):
        add(("ym", j), 2 + j, "ymix_ready", j + 1)
    for j in range(4):
        add(("yc", j), [0, 1, 6, 7][j], "mix_ready", j + 1)
    for t in range(2):
        for c in range(2):
            add(("ho", t, c), 4 + 2 * t + c, "h1_ready", 2 * t + c + 1)
    for t in range(2):
        for c in range(2):
            add(("xt", t, c), 2 * t + c, "xnT_ready", 2 * t + c + 1)
    add("lgt", 4, "lgT_ready", 1)
    add("lg", 5, "logits_ready", 1)
    add("rank", 6, "rank_ready", 1)
    add("cnt", 7, "cnt_ready", 1)
    add("gt", 4, "gateT_ready", 1)
    return plan, turns


def layer(nc, a, out):
    plan, turns = bank_plan()
    ctx = ExitStack()
    with ctx:
        named = {}

        def sem(name):
            named[name] = ctx.enter_context(nc.semaphore(name))
            return named[name]

        GU, DN, W = 16384, 8192, 12248
        arena = ctx.enter_context(nc.sbuf_tensor("arena", [P, 2 * GU + DN + W], F32))
        psum = ctx.enter_context(nc.psum_tensor("psum", [P, 8, 512], F32))

        def words(at, n):
            return arena[:, at:at + n]

        def grid(at, x, y):
            return words(at, x * y).rearrange("p (x y) -> p x y", x=x)

        A0, B0, D0, W0 = 0, GU, 2 * GU, 2 * GU + DN
        gu = [[words((A0, B0)[i] + 2048 * k, 2048) for k in range(KD)] for i in range(2)]
        dn = [grid(D0 + 2048 * i, 2, 1024) for i in range(4)]

        RING = 6
        win = [grid(A0 + 2048 * s, KD, 256) for s in range(RING)]
        at = A0 + 2048 * RING
        hnT = grid(at, KD, L); at += KD * L
        qnT = grid(at, 2, SEQ); at += 2 * SEQ
        ckvn = words(at, L); at += L
        sqq = grid(at, 2, SEQ); at += 2 * SEQ
        sqk = words(at, L); at += L
        kpeT = words(at, L)
        wo = grid(D0, 4, D)
        pw2 = grid(D0 + 4096, 4, D)
        xpos = grid(B0, 3, D)
        junk = words(B0 + 4096, D)
        head_sq = [words(B0, 3 * H * HD), words(B0 + 3 * H * HD, 2 * H * HD)]
        gT = grid(B0, 16, SEQ)
        mixT = grid(B0 + 4096, KD, SEQ)
        hc = grid(B0 + 6144, CT, PAD + L)
        sqc = grid(B0 + 6144, CT, SEQ)
        half_mix = grid(B0 + 6144, 2, SEQ)
        rsb = words(B0 + 7296, L)
        rsb2 = words(B0 + 7296 + L, SEQ)
        h1 = grid(B0, 2, D)
        xn = grid(B0 + 2048, 2, D)
        xnT = grid(B0 + 4096, KD, SEQ)
        rest = grid(B0 + 6144, 2, D)
        at = B0 + 8192
        q = grid(at, 2, H * HD); at += 2 * H * HD
        kk = grid(at, 3, H * HD); at += 3 * H * HD
        v = grid(at, 3, H * VD); at += 3 * H * VD
        wqb = grid(at, 2, H * HD); at += 2 * H * HD
        wkvb = words(at, H * 128)
        rows = grid(B0 + 8192, 2, P)
        wout = grid(B0 + 8192, KD, D)
        const = words(W0, C_END)
        at = W0 + C_END
        par = words(at, R_END); at += R_END
        dw = words(at, TAPS * CT); at += TAPS * CT
        small = words(at, 384); at += 384
        WB = at
        acc = grid(at, CT, SEQ); at += CT * SEQ
        xres = grid(at, 2, D)
        qT = grid(at, H, SEQ); at += H * SEQ
        kT = grid(at, H, L); at += H * L
        oT = grid(at, 4, SEQ); at += 4 * SEQ
        sig = grid(at, 2, L); at += 2 * L
        tmp = words(at, 2304)
        prob = grid(at, 2, L)
        probT = grid(at + 2 * L, 2, 384)
        sm = grid(at + 2 * L + 768, 2, L); at += 2304
        assert at <= W0 + W
        at = WB
        xn3 = words(at, 3072).bitcast(BF16).rearrange("p (t s d) -> p t s d", t=2, s=3); at += 3072
        biasgu = words(at, 2 * FF); at += 2 * FF
        wp = [grid(at + 384 * i, 2, 192) for i in range(2)]; at += 768
        ph = [words(at + 64 * i, 64).bitcast(BF16).rearrange("p (t s) -> p t s", t=2) for i in range(2)]; at += 128
        pick = [words(at + 64 * i, 64) for i in range(2)]; at += 128
        bdown = words(at, D)
        xe = [grid(at + 512 * i, KD, SLOTS) for i in range(2)]; at += 1024
        sT = [grid(at + 512 * i, 4, P) for i in range(2)]; at += 1024
        fnw = words(at, D)
        rwt = grid(at + D, KD, E)
        lgT = words(at + D + 256, SEQ)
        tk = words(at + D + 512, 512)
        g_s = words(at, 512); at += 512
        sg = words(at, 512)
        aT = grid(at, 4, P); at += 512
        a_s = words(at, 512); at += 512
        y_s = words(at, 512); at += 512
        assert at <= W0 + W
        ov_s = words(at, 320)
        assert at + 320 <= W0 + W
        ysb = grid(A0, 4, 512)

        ident, ones = const[:, C_ID:C_ID + P], const[:, C_ONE:C_ONE + P]
        tri, iota = const[:, C_TRI:C_TRI + P], const[:, C_IOTA:C_IOTA + 256]

        def cols(i, n):
            return small[:, i:i + n]

        ssx, rsx, knc, qnc, knr, qnr, hs = cols(0, 3), cols(3, 3), cols(6, 1), cols(7, 1), cols(8, 32), cols(40, 32), \
            cols(72, 24)
        mx, nmx, psm, prs = cols(96, 2), cols(98, 2), cols(100, 2), cols(102, 2)
        rbc, ssh, rsh, ovn = cols(104, 1), cols(105, 2), cols(107, 2), cols(109, 1)
        ovni = cols(110, 1).bitcast(I32)
        hsq, warm = cols(111, 16), cols(127, 1)
        qscale, qnscale = cols(320, 16), cols(336, 16)
        rankp, gate, maskt = (cols(i, 64).rearrange("p (t e) -> p t e", t=2) for i in (128, 192, 256))
        ovf = cols(320, 16)
        ove, ovb = cols(336, 16).bitcast(I32), cols(352, 16).bitcast(I32)

        bank_full = [sem(f"bank_full{b}") for b in range(8)]
        dve_step, act_step, pool_step = sem("dve_step"), sem("act_step"), sem("pool_step")
        in_const, in_rows, in_cols = sem("in_const"), sem("in_rows"), sem("in_cols")
        in_x = [sem(f"in_x{t}") for t in range(3)]
        in_win = [sem(f"in_win{s}") for s in range(RING)]
        in_wqb, in_wkvb, in_wo, in_pw2 = sem("in_wqb"), sem("in_wkvb"), sem("in_wo"), sem("in_pw2")
        in_wout, in_res, in_router, in_bias = sem("in_wout"), sem("in_res"), sem("in_router"), sem("in_bias")
        in_gu = [[sem(f"in_gu{i}_{k}") for k in range(KD)] for i in range(2)]
        in_dn = [sem(f"in_dn{i}") for i in range(4)]
        for name in ("cols_clear pads_clear hcpad_clear bias_clear par_ready xss_ready xvar_ready xroot_ready xs_ready hn_ready "
                     "squares kpe_ready lvar_ready lroot_ready lat_ready csig_ready convin_ready v_ready "
                     "kraw_ready qraw_ready ksq_ready qsq_ready khvar_ready khroot_ready qhvar_ready qhroot_ready k_ready q_ready "
                     "kT_ready qT_ready max_ready exp_ready prob_ready probT_ready gT_ready gates_ready oT_ready conv_ready "
                     "lncent_ready lnsq_ready lnvar_ready lnroot_ready lny_ready silu_ready ymix_ready mix_ready "
                     "h1_ready h1ss_ready h1var_ready h1root_ready xn_ready xnT_ready hi_ready rest_ready "
                     "mid_ready split_ready lgT_ready logits_ready top_ready exp4_ready mask_ready rank_ready "
                     "cnt_ready gate_ready gateT_ready front_done overflow_ready gu_done dn_done built gathered "
                     "xe_ready turned sT_ready g_ready a_step sg_ready act_ready aT_done aT_ready y_ready scattered "
                     "fin_act fin_dve stored").split():
            sem(name)
        S = type("Semaphores", (), named)

        block = ctx.enter_context(nc.Block())

        TR = [P, P, META]
        pieces = ["kv", "q"] + [("c", j) for j in range(CT)] + [("g", j) for j in range(8)]
        piece_at = {name: (i % RING, 32 * (i // RING + 1)) for i, name in enumerate(pieces)}
        piece_used = {"kv": (S.kpe_ready, 1), "q": (S.squares, 2)}
        piece_used.update({("c", j): (S.csig_ready, j + 1) for j in range(CT)})
        piece_used.update({("g", j): (S.gT_ready, 2 * j + 2) for j in range(8)})
        w_in, x = a["w_in"][0], a["x"][0]
        weights_gu, weights_dn = a["w_gate_up"][0], a["w_down"][0]

        def span(t):
            return META + P * (t + 1)

        @block.sync
        def _(sp):
            sp.dma_start(xpos[0:META, 0, :], a["meta_tokens"]).then_inc(in_x[0], 16)
            sp.dma_start(xpos[META:P, 0, :], x[0:P - META, :]).then_inc(in_x[0], 16)
            sp.dma_start(xpos[:, 1, :], x[P - META:2 * P - META, :]).then_inc(in_x[1], 16)
            sp.dma_start(xpos[0:META, 2, :], x[2 * P - META:SEQ, :]).then_inc(in_x[2], 16)
            sp.dma_start(const, a["const"]).then_inc(in_const, 16)

            def load_win(i):
                slot, name = i % RING, pieces[i]
                if i >= RING:
                    sp.wait_ge(*piece_used[pieces[i - RING]])
                src = w_in.rearrange("(k p) c -> p k c", p=P)
                if name == "kv":
                    parts = [(0, COL_KV, KVL), (KVL, COL_KV + KVL, ROPE)]
                elif name == "q":
                    parts = [(0, COL_Q, P), (P, COL_Q + P, P)]
                elif name[0] == "c":
                    parts = [(0, P * name[1], P), (P, CONV + P * name[1], P)]
                else:
                    parts = [(0, COL_G + 256 * name[1], P), (P, COL_G + 256 * name[1] + P, P)]
                for to, frm, n in parts:
                    sp.dma_start(win[slot][:, :, to:to + n], src[:, :, frm:frm + n]).then_inc(in_win[slot], 16)

            load_win(0)
            for src, row, n in [("attn_norm_w", R_ATTN, 8), ("conv_dw_b", R_DWB, 4), ("conv_ln_w", R_LNW, 4),
                                ("conv_ln_b", R_LNB, 4), ("q_a_norm_w", R_QA, 2), ("kv_a_norm_w", R_KVA, 1),
                                ("gate_b", R_GB, 16)]:
                sp.dma_start(rows[row:row + n, 0, :], a[src][0].rearrange("(r c) -> r c", c=P)
                            ).then_inc(in_rows, 16)
            sp.dma_start(rows[0:TAPS * CT, 1, :], a["conv_dw_w"][0].rearrange("j (c p) -> (j c) p", p=P)
                         ).then_inc(in_rows, 16)
            for i in range(1, 4):
                load_win(i)
            sp.wait_ge(S.par_ready, 1)
            sp.dma_start(wkvb, a["w_kv_b"][0]).then_inc(in_wkvb, 16)
            sp.dma_start(wqb, a["w_q_b"][0].rearrange("(k p) c -> p k c", p=P)).then_inc(in_wqb, 16)
            for i in range(4, 10):
                load_win(i)
            sp.dma_start(wo, a["w_o_mla"][0].rearrange("(k p) c -> p k c", p=P)).then_inc(in_wo, 16)
            sp.dma_start(pw2, a["conv_pw2_w"][0].rearrange("(k p) c -> p k c", p=P)).then_inc(in_pw2, 16)
            for i in range(10, len(pieces)):
                load_win(i)

            def load_gu(e, i, k):
                if isinstance(e, int):
                    src = weights_gu[e, k * P:(k + 1) * P, :]
                else:
                    src = weights_gu[bass.ds(e, 1), k * P:(k + 1) * P, :].rearrange("a p c -> (a p) c")
                sp.dma_start(gu[i][k], src).then_inc(in_gu[i][k], 16)

            def load_dn(e, i):
                src = weights_dn[e:e + 1] if isinstance(e, int) else weights_dn[bass.ds(e, 1)]
                src = src[:, 2 * i * P:(2 * i + 2) * P, :].rearrange("a (k p) c -> p (a k) c", p=P)
                sp.dma_start(dn[i], src).then_inc(in_dn[i], 16)

            for k in range(2, 6):
                sp.wait_ge(*piece_used["g", k])
                load_gu(0, 0, k)
            sp.wait_ge(S.oT_ready, 4)
            sp.dma_start(wout, a["w_out"][0].rearrange("(k p) c -> p k c", p=P)).then_inc(in_wout, 16)
            for t in range(2):
                sp.dma_start(xres[:, t, :], x[t * P:(t + 1) * P, :]).then_inc(in_res, 16)
            sp.dma_start(fnw, a["ffn_norm_w"][0].partition_broadcast(P)
                         ).then_inc(in_router, 16)
            sp.dma_start(rwt, a["router_w"][0].rearrange("(k p) e -> p k e", p=P)).then_inc(in_router, 16)
            for k in (0, 1, 6, 7):
                load_gu(0, 0, k)
            sp.wait_ge(S.mix_ready, 4)
            for i in range(4):
                load_dn(0, i)
            sp.wait_ge(S.h1_ready, 4)
            for k in range(4, 8):
                load_gu(1, 1, k)
            sp.wait_ge(S.front_done, 1)
            for k in range(4):
                load_gu(1, 1, k)
            def next_gu(n, u):
                for k in range(KD):
                    sp.wait_ge(S.gu_done, 8 * (n - 2) + (k + 1))
                    load_gu(n, u, k)

            def next_dn(n):
                for i in range(4):
                    sp.wait_ge(S.dn_done, 4 * (n - 1) + (i + 1))
                    load_dn(n, i)

            EARLY = 6
            with sp.Fori(0, EARLY // 2) as it:
                for u in range(2):
                    next_gu(2 * it + (2 + u), u)
                    next_dn(2 * it + (1 + u))
            next_dn(EARLY + 1)
            with sp.Fori(0, (E - EARLY - 2) // 2) as it:
                for u in range(2):
                    next_gu(2 * it + (EARLY + 2 + u), u)
                    next_dn(2 * it + (EARLY + 2 + u))
            sp.wait_ge(S.overflow_ready, 1)
            count = sp.value_load(ovni[0:1, :], min_val=0, max_val=EXTRA)
            with sp.If(count > 0):
                with sp.Fori(0, count) as j:
                    e = sp.value_load(ove[0:1, bass.ds(j, 1)], min_val=0, max_val=E - 1)
                    sp.wait_ge(S.gu_done, 8 * j + 8 * E)
                    for k in range(KD):
                        load_gu(e, 0, k)
                    sp.wait_ge(S.dn_done, 4 * j + 4 * E)
                    for i in range(4):
                        load_dn(e, i)
            for i in range(4):
                sp.wait_ge(S.fin_act if i < 2 else S.fin_dve, i % 2 + 1)
                sp.dma_start(out[0, (i // 2) * P:(i // 2 + 1) * P, (i % 2) * 512:(i % 2 + 1) * 512], ysb[:, i, :]
                             ).then_inc(S.stored, 16)
            sp.wait_ge(S.stored, 64)

        @block.gpsimd
        def _(pool):
            nc.gpsimd.memset(small, 1.0).then_inc(S.cols_clear, 1)
            pool.wait_ge(S.cols_clear, 1)
            with nc.allow_non_contiguous_dma(reason="one value a partition"):
                for to, src in [(knc, "k_norm_w"), (qnc, "q_norm_w")]:
                    pool.dma_start(to[0:NOPE, :], a[src][0, 0:NOPE].rearrange("(p a) -> p a", a=1)
                                   ).then_inc(in_cols, 16)
                pool.dma_start(rbc[0:E, :], a["router_b"][0].rearrange("(p a) -> p a", a=1)).then_inc(in_cols, 16)
            for to, src in [(knr, "k_norm_w"), (qnr, "q_norm_w")]:
                pool.dma_start(to, a[src][0, NOPE:HD].partition_broadcast(P)
                               ).then_inc(in_cols, 16)
            nc.gpsimd.memset(hc[:, :, 0:PAD], 0.0).then_inc(S.pads_clear, 1)
            pool.wait_ge(S.par_ready, 1)
            nc.gpsimd.memset(kk[:, 2, :], 0.0).then_inc(S.pads_clear, 1)
            pool.wait_ge(S.h1_ready, 4)
            pool.dma_start(bdown[0:E, :], a["b_down"][0]).then_inc(in_bias, 16)
            for t in range(2):
                pool.wait_ge(S.xn_ready, t + 1)
                nc.gpsimd.tensor_copy(xn3[:, t, 0, :], xn[:, t, :]).then_inc(S.hi_ready, 1)
            for t in range(2):
                pool.wait_ge(S.rest_ready, t + 1)
                nc.gpsimd.tensor_copy(xn3[:, t, 1, :], rest[:, t, :]).then_inc(S.mid_ready, 1)
            pool.wait_ge(S.bias_clear, 1)
            pool.dma_start(biasgu[0:E, :], a["b_gate_up"][0]).then_inc(in_bias, 16)

        @block.tensor
        def _(pe):
            mm = nc.tensor.matmul

            def fill(job):
                bank, turn, _ = plan[job]
                if turn:
                    release, value = plan[turns[bank][turn - 1]][2]
                    pe.wait_ge(named[release], value)
                return psum[:, bank, :]

            def filled(job, ins):
                ins.then_inc(bank_full[plan[job][0]], 1)

            pe.wait_ge(in_rows, 16 * 8)
            pe.wait_ge(in_const, 16)
            b = fill("par")
            nc.tensor.transpose(b[:, 0:R_END], rows[0:R_END, 0, :], ident[0:R_END, 0:R_END])
            filled("par", nc.tensor.transpose(b[:, 128:128 + TAPS * CT], rows[0:TAPS * CT, 1, :],
                                              ident[0:TAPS * CT, 0:TAPS * CT]))
            for t in range(3):
                pe.wait_ge(S.xs_ready, t + 1)
                r = TR[t]
                for c in range(2 if t < 2 else 1):
                    b = fill(("hn", t, c))
                    for k in range(4 if t < 2 else 8):
                        kt = 4 * c + k
                        last = nc.tensor.transpose(b[:, r * k:r * (k + 1)], xpos[0:r, t, kt * P:(kt + 1) * P],
                                                   ident[0:r, 0:r])
                    filled(("hn", t, c), last)
            pe.wait_ge(S.hn_ready, 5)

            def project(b, piece, c0, m, n0, n):
                slot, value = piece_at[piece]
                pe.wait_ge(in_win[slot], value)
                for k in range(KD):
                    last = mm(b, win[slot][:, k, c0:c0 + m], hnT[:, k, n0:n0 + n], start=(k == 0),
                              stop=(k == KD - 1))
                return last

            filled("ckv", project(fill("ckv")[:, 0:L], "kv", 0, P, 0, L))
            filled("kpe", project(fill("kpe")[0:ROPE, 0:L], "kv", P, ROPE, 0, L))
            b = fill("q")
            for j in range(2):
                last = project(b[:, j * SEQ:(j + 1) * SEQ], "q", P * j, P, META, SEQ)
            filled("q", last)

            def conv_tile(j):
                filled(("ca", j), project(fill(("ca", j))[:, 0:L], ("c", j), 0, P, 0, L))
                filled(("cg", j), project(fill(("cg", j))[:, 0:L], ("c", j), P, P, 0, L))

            conv_tile(0)
            pe.wait_ge(S.squares, 1)
            filled("ssk", mm(fill("ssk")[:, 0:L], ones, sqk, start=True, stop=True))
            pe.wait_ge(S.squares, 2)
            b = fill("ssq")[:, 0:SEQ]
            for j in range(2):
                last = mm(b, ones, sqq[:, j, :], start=(j == 0), stop=(j == 1))
            filled("ssq", last)
            conv_tile(1)
            pe.wait_ge(in_wkvb, 16)
            pe.wait_ge(S.lat_ready, 1)
            for t in range(3):
                for c in range(2):
                    filled(("kvb", t, c), mm(fill(("kvb", t, c))[0:TR[t], :], ckvn[:, t * P:t * P + TR[t]],
                                             wkvb[:, c * 512:(c + 1) * 512], start=True, stop=True))
            pe.wait_ge(S.kpe_ready, 1)
            b = fill("kpet")
            for t in range(3):
                last = nc.tensor.transpose(b[0:TR[t], t * ROPE:(t + 1) * ROPE], kpeT[0:ROPE, t * P:t * P + TR[t]],
                                           ident[0:ROPE, 0:ROPE])
            filled("kpet", last)
            conv_tile(2)
            pe.wait_ge(in_wqb, 16)
            pe.wait_ge(S.lat_ready, 2)
            for t in range(2):
                for c in range(2):
                    b = fill(("qb", t, c))[:, 0:384]
                    for k in range(2):
                        last = mm(b, qnT[:, k, t * P:(t + 1) * P], wqb[:, k, c * 384:(c + 1) * 384],
                                  start=(k == 0), stop=(k == 1))
                    filled(("qb", t, c), last)
            conv_tile(3)
            pe.wait_ge(S.k_ready, 1)
            for t in range(3):
                r = TR[t]
                for c in range(2 if t < 2 else 1):
                    b = fill(("kt", t, c))
                    for i in range(4 if t < 2 else 8):
                        h = 4 * c + i
                        last = nc.tensor.transpose(b[0:HD, r * i:r * (i + 1)], kk[0:r, t, h * HD:(h + 1) * HD],
                                                   ident[0:r, 0:r])
                    filled(("kt", t, c), last)
            pe.wait_ge(S.q_ready, 1)
            for t in range(2):
                for c in range(2):
                    b = fill(("qt", t, c))
                    for i in range(4):
                        h = 4 * c + i
                        last = nc.tensor.transpose(b[0:HD, P * i:P * (i + 1)], q[:, t, h * HD:(h + 1) * HD], ident)
                    filled(("qt", t, c), last)

            def scores(s):
                h, t = s // 2, s % 2
                filled(("s", s), mm(fill(("s", s))[:, 0:span(t)], qT[0:HD, h, t * P:(t + 1) * P],
                                    kT[0:HD, h, 0:span(t)], start=True, stop=True))

            pe.wait_ge(S.kT_ready, 5)
            pe.wait_ge(S.qT_ready, 4)
            scores(0)
            def values(s):
                h, t = s // 2, s % 2
                if s % 4 == 0:
                    fill(("ot", s // 4))
                b = psum[64 * (h % 2):64 * (h % 2) + VD, plan[("ot", s // 4)][0], t * P:(t + 1) * P]
                pe.wait_ge(S.probT_ready, s + 1)
                tiles = key_tiles(t)
                for i, (c0, n) in enumerate(tiles):
                    last = mm(b, v[0:n, c0 // P, h * VD:(h + 1) * VD], probT[0:n, s % 2, i * P:(i + 1) * P],
                              start=(i == 0), stop=(i == len(tiles) - 1))
                if s % 4 == 3:
                    filled(("ot", s // 4), last)

            def key_tiles(t):
                return [(c0, min(P, span(t) - c0)) for c0 in range(0, span(t), P)]

            for s in range(2 * H):
                b = fill(("gate", s))[:, 0:SEQ]
                slot, value = piece_at["g", s // 2]
                pe.wait_ge(in_win[slot], value)
                for k in range(KD):
                    if k == 2 and s:
                        values(s - 1)
                    last = mm(b, win[slot][:, k, P * (s % 2):P * (s % 2) + P], hnT[:, k, META:META + SEQ],
                              start=(k == 0), stop=(k == KD - 1))
                filled(("gate", s), last)
                pe.wait_ge(S.prob_ready, s + 1)
                b = fill(("pt", s))
                for i, (c0, n) in enumerate(key_tiles(s % 2)):
                    last = nc.tensor.transpose(b[0:n, i * P:(i + 1) * P], prob[:, s % 2, c0:c0 + n], ident)
                filled(("pt", s), last)
                if s + 1 < 2 * H:
                    scores(s + 1)
            values(2 * H - 1)
            pe.wait_ge(S.conv_ready, 1)
            b = fill("lnmu")[:, 0:SEQ]
            for j in range(CT):
                last = mm(b, ones, acc[:, j, :], start=(j == 0), stop=(j == CT - 1))
            filled("lnmu", last)

            def mixer(job, w, act_t):
                b = fill(job)
                for i in range(2):
                    m = 2 * job[1] + i
                    for k in range(4):
                        last = mm(b[:, i * SEQ:(i + 1) * SEQ], w[:, k, m * P:(m + 1) * P], act_t[:, k, :],
                                  start=(k == 0), stop=(k == 3))
                filled(job, last)

            pe.wait_ge(in_wo, 16)
            pe.wait_ge(S.oT_ready, 4)
            for j in range(4):
                if j == 2:
                    pe.wait_ge(S.lnsq_ready, 1)
                    b = fill("lnvar")[:, 0:SEQ]
                    for c in range(CT):
                        last = mm(b, ones, sqc[:, c, :], start=(c == 0), stop=(c == CT - 1))
                    filled("lnvar", last)
                mixer(("ym", j), wo, oT)
            pe.wait_ge(in_pw2, 16)
            pe.wait_ge(S.silu_ready, 1)
            for j in range(4):
                mixer(("yc", j), pw2, acc)
            pe.wait_ge(in_wout, 16)
            held = {(t, c): fill(("ho", t, c)) for t in range(2) for c in range(2)}
            for k in range(KD):
                pe.wait_ge(S.mix_ready, k // 2 + 1)
                for t in range(2):
                    for c in range(2):
                        last = mm(held[t, c], mixT[:, k, t * P:(t + 1) * P], wout[:, k, c * 512:(c + 1) * 512],
                                  start=(k == 0), stop=(k == KD - 1))
                        if k == KD - 1:
                            filled(("ho", t, c), last)
            for t in range(2):
                pe.wait_ge(S.xn_ready, t + 1)
                for c in range(2):
                    b = fill(("xt", t, c))
                    for k in range(4):
                        kt = 4 * c + k
                        last = nc.tensor.transpose(b[:, k * P:(k + 1) * P], xn[:, t, kt * P:(kt + 1) * P], ident)
                    filled(("xt", t, c), last)
            pe.wait_ge(in_router, 32)
            pe.wait_ge(S.xnT_ready, 4)
            b = fill("lgt")[0:E, 0:SEQ]
            for k in range(KD):
                last = mm(b, rwt[:, k, :], xnT[:, k, :], start=(k == 0), stop=(k == KD - 1))
            filled("lgt", last)
            pe.wait_ge(S.lgT_ready, 1)
            b = fill("lg")
            for t in range(2):
                last = nc.tensor.transpose(b[:, t * E:(t + 1) * E], lgT[0:E, t * P:(t + 1) * P], ident[0:E, 0:E])
            filled("lg", last)
            pe.wait_ge(S.mask_ready, 1)
            b = fill("rank")
            mm(b[:, 0:E], tri, maskt[:, 0, :], start=True, stop=True)
            mm(b[:, E:2 * E], tri, maskt[:, 1, :], start=True, stop=False)
            filled("rank", mm(b[:, E:2 * E], ones, maskt[:, 0, :], start=False, stop=True))
            b = fill("cnt")
            mm(b[:, 0:E], ones, maskt[:, 0, :], start=True, stop=False)
            filled("cnt", mm(b[:, 0:E], ones, maskt[:, 1, :], start=False, stop=True))
            pe.wait_ge(S.gate_ready, 1)
            b = fill("gt")
            for t in range(2):
                last = nc.tensor.transpose(b[0:E, t * P:(t + 1) * P], gate[:, t, :], ident)
            filled("gt", last)

            def total(t, c):
                return psum[:, 2 * t + c, :]

            for bank in range(4):
                release, value = plan[turns[bank][-1]][2]
                pe.wait_ge(named[release], value)
            for t in range(2):
                for c in range(2):
                    mm(total(t, c), ident, h1[:, t, c * 512:(c + 1) * 512], start=True, stop=False,
                       skip_group_check=True)
            pe.wait_ge(S.gateT_ready, 1)
            pe.wait_ge(in_bias, 32)
            pe.wait_ge(S.split_ready, 2)
            for t in range(2):
                for c in range(2):
                    last = mm(total(t, c), lgT[0:E, t * P:(t + 1) * P], bdown[0:E, c * 512:(c + 1) * 512],
                              start=False, stop=False, skip_group_check=True)
            last.then_inc(S.front_done, 1)
            for bank in range(4, 8):
                release, value = plan[turns[bank][-1]][2]
                pe.wait_ge(named[release], value)
            G, U, X, Y = (psum[:, bank, :] for bank in range(4, 8))

            def gather(n, i):
                pe.wait_ge(S.built, n + 1)
                if not isinstance(n, int) or n:
                    pe.wait_ge(S.sT_ready, n)
                for k in range(KD):
                    for t in range(2):
                        for part in range(3):
                            last = mm(X[:, k * SLOTS:(k + 1) * SLOTS], xn3[:, t, part, k * P:(k + 1) * P],
                                      ph[i][:, t, :], start=(t == 0 and part == 0), stop=(t == 1 and part == 2))
                last.then_inc(S.gathered, 1)

            def turn(n, i):
                pe.wait_ge(S.xe_ready, n + 1)
                for c in range(2):
                    for t in range(2):
                        j = 2 * c + t
                        last = nc.tensor.transpose(X[:, j * P:(j + 1) * P], wp[i][:, t, 64 - 64 * c:192 - 64 * c],
                                                   ident)
                last.then_inc(S.turned, 1)

            def gate_up(n, i, loads):
                pe.wait_ge(S.xe_ready, n + 1)
                for half in range(2):
                    for o, b in ((0, G), (FF, U)):
                        mm(b[64 * half:64 * half + 64, :], pick[i],
                           biasgu[:, o + half * 512:o + half * 512 + 512], start=True, stop=False)
                for k in range(KD):
                    pe.wait_ge(in_gu[i][k], loads)
                    for o, b in ((0, G), (FF, U)):
                        for half in range(2):
                            last = mm(b[64 * half:64 * half + 64, :], xe[i][:, k, :],
                                      gu[i][k][:, o + half * 512:o + half * 512 + 512], start=False,
                                      stop=(k == KD - 1))
                    last.then_inc(S.gu_done, 1)

            def turn_act(n):
                pe.wait_ge(S.act_ready, n + 1)
                for c in range(4):
                    last = nc.tensor.transpose(Y[:, c * P:(c + 1) * P], a_s[:, c * P:(c + 1) * P], ident)
                last.then_inc(S.aT_done, 1)

            def down(n, loads):
                pe.wait_ge(S.aT_ready, n + 1)
                for i in range(4):
                    pe.wait_ge(in_dn[i], loads)
                    for u in range(2):
                        k = 2 * i + u
                        for c in range(2):
                            last = mm(Y[64 * c:64 * c + 64, :], aT[:, k % 4, 64 * (k // 4):64 * (k // 4) + 64],
                                      dn[i][:, u, c * 512:(c + 1) * 512], start=(k == 0), stop=(k == KD - 1))
                    last.then_inc(S.dn_done, 1)

            def scatter(n, i):
                pe.wait_ge(S.y_ready, n + 1)
                for t in range(2):
                    for c in range(2):
                        last = mm(total(t, c), sT[i][:, 2 * c + t, :], y_s, start=False, stop=False,
                                  skip_group_check=True)
                last.then_inc(S.scattered, 1)

            def item(n, i, gu_loads, dn_loads, first=False, final=False):
                gate_up(n, i, gu_loads)
                if not final:
                    gather(n + 1, 1 - i)
                if not first:
                    scatter(n - 1, 1 - i)
                if not final:
                    turn(n + 1, 1 - i)
                turn_act(n)
                down(n, dn_loads)

            gather(0, 0)
            turn(0, 0)
            item(0, 0, 16, 16, first=True)
            with pe.Fori(0, E // 2 - 1) as it:
                item(2 * it + 1, 1, 16 * it + 16, 32 * it + 32)
                item(2 * it + 2, 0, 16 * it + 32, 32 * it + 48)
            item(E - 1, 1, 16 * (E // 2), 16 * E, final=True)
            scatter(E - 1, 1)
            pe.wait_ge(S.overflow_ready, 1)
            count = pe.value_load(ovni[0:1, :], min_val=0, max_val=EXTRA)
            with pe.If(count > 0):
                with pe.Fori(0, count) as j:
                    n = j + E
                    gather(n, 0)
                    turn(n, 0)
                    gate_up(n, 0, 16 * j + 16 * (E // 2 + 1))
                    turn_act(n)
                    down(n, 16 * j + 16 * (E + 1))
                    scatter(n, 0)

        @block.scalar
        def _(act):
            f = nc.scalar.activation

            def full(job):
                bank, turn, _ = plan[job]
                act.wait_ge(bank_full[bank], turn + 1)
                return psum[:, bank, :]

            act.wait_ge(S.cols_clear, 1)
            f(warm, warm, ACT.Sqrt)
            for t in range(3):
                act.wait_ge(in_x[t], 32 if t == 0 else 16)
                r = TR[t]
                f(junk[0:r, :], xpos[0:r, t, :], ACT.Square, accum_out=ssx[0:r, t:t + 1]).then_inc(S.xss_ready, 1)
                act.wait_ge(S.xvar_ready, t + 1)
                f(rsx[:, t:t + 1], ssx[:, t:t + 1], ACT.Sqrt).then_inc(S.xroot_ready, 1)
            b = full("par")
            nc.scalar.copy(par, b[:, 0:R_END])
            nc.scalar.copy(dw, b[:, 128:128 + TAPS * CT]).then_inc(S.par_ready, 1)
            b = full("ckv")
            nc.scalar.copy(ckvn, b[:, 0:L])
            f(sqk, b[:, 0:L], ACT.Square).then_inc(S.squares, 1)
            nc.scalar.copy(kpeT[0:ROPE, :], full("kpe")[0:ROPE, 0:L]).then_inc(S.kpe_ready, 1)
            b = full("q").rearrange("p (j n) -> p j n", j=2)
            nc.scalar.copy(qnT, b)
            f(sqq, b, ACT.Square).then_inc(S.squares, 1)

            def conv_gate(j):
                if j >= 2:
                    act.wait_ge(S.convin_ready, j - 1)
                f(sig[:, j % 2, :], full(("cg", j))[:, 0:L], ACT.Sigmoid).then_inc(S.csig_ready, 1)

            conv_gate(0)
            act.wait_ge(S.lvar_ready, 1)
            f(rsb, rsb, ACT.Sqrt).then_inc(S.lroot_ready, 1)
            act.wait_ge(S.lvar_ready, 2)
            f(rsb2, rsb2, ACT.Sqrt).then_inc(S.lroot_ready, 1)
            conv_gate(1)
            act.wait_ge(S.pads_clear, 2)
            for t in range(3):
                for c in range(2):
                    b = full(("kvb", t, c))[0:TR[t], :].rearrange("p (h d) -> p h d", h=4)
                    kv_heads = kk[0:TR[t], t, :].rearrange("p (h d) -> p h d", h=H)[:, 4 * c:4 * c + 4, :]
                    v_heads = v[0:TR[t], t, :].rearrange("p (h d) -> p h d", h=H)[:, 4 * c:4 * c + 4, :]
                    nc.scalar.copy(kv_heads[:, :, 0:NOPE], b[:, :, 0:NOPE])
                    nc.scalar.copy(v_heads, b[:, :, NOPE:NOPE + VD]).then_inc(S.v_ready, 1)
            b = full("kpet")
            for t in range(3):
                kv_heads = kk[0:TR[t], t, :].rearrange("p (h d) -> p h d", h=H)
                last = nc.scalar.copy(kv_heads[:, :, NOPE:HD], b[0:TR[t], t * ROPE:(t + 1) * ROPE].unsqueeze(1)
                                      .to_broadcast([TR[t], H, ROPE]))
            last.then_inc(S.kraw_ready, 1)
            act.wait_ge(S.kraw_ready, 1)
            f(head_sq[0], kk.rearrange("p t c -> p (t c)"), ACT.Square).then_inc(S.ksq_ready, 1)
            conv_gate(2)
            act.wait_ge(S.khvar_ready, 1)
            f(hs, hs, ACT.Sqrt).then_inc(S.khroot_ready, 1)
            for t in range(2):
                for c in range(2):
                    nc.scalar.copy(q[:, t, c * 384:(c + 1) * 384], full(("qb", t, c))[:, 0:384]
                                   ).then_inc(S.qraw_ready, 1)
            act.wait_ge(S.qraw_ready, 4)
            f(head_sq[1], q.rearrange("p t c -> p (t c)"), ACT.Square).then_inc(S.qsq_ready, 1)
            conv_gate(3)
            act.wait_ge(in_cols, 80)
            for t in range(3):
                r = TR[t]
                for c in range(2 if t < 2 else 1):
                    n = 4 if t < 2 else 8
                    b = full(("kt", t, c))[0:HD, 0:n * r].rearrange("p (h j) -> p h j", h=n)
                    f(kT[0:HD, 4 * c:4 * c + n, t * P:t * P + r], b, ACT.Copy, scale=knc[0:HD, :]
                      ).then_inc(S.kT_ready, 1)
            act.wait_ge(S.qhvar_ready, 1)
            f(hsq, hsq, ACT.Sqrt).then_inc(S.qhroot_ready, 1)

            def heads_out(j):
                nc.scalar.copy(oT[:, j, :], full(("ot", j))[:, 0:SEQ]).then_inc(S.oT_ready, 1)

            for s in range(2 * H):
                h, t = s // 2, s % 2
                act.wait_ge(S.max_ready, s + 1)
                f(prob[:, t, 0:span(t)], sm[:, t, 0:span(t)], ACT.Exp, bias=nmx[:, t:t + 1],
                  scale=qscale[:, t * H + h:t * H + h + 1], accum_out=psm[:, t:t + 1]).then_inc(S.exp_ready, 1)
                f(gT[:, s, :], full(("gate", s))[:, 0:SEQ], ACT.Identity, bias=par[:, R_GB + s:R_GB + s + 1]
                  ).then_inc(S.gT_ready, 1)
                if s and s % 4 == 0:
                    heads_out(s // 4 - 1)
                b = full(("pt", s))
                n = span(t) // P
                nc.scalar.copy(probT[:, t, 0:n * P], b[:, 0:n * P])
                nc.scalar.copy(probT[0:META, t, n * P:(n + 1) * P], b[0:META, n * P:(n + 1) * P]
                               ).then_inc(S.probT_ready, 1)
            heads_out(3)
            act.wait_ge(S.gT_ready, 2 * H)
            f(gT[:, 8:16, :], gT[:, 8:16, :], ACT.Sigmoid).then_inc(S.gates_ready, 1)
            act.wait_ge(S.lncent_ready, 1)
            f(sqc, acc, ACT.Square).then_inc(S.lnsq_ready, 1)
            f(gT[:, 0:8, :], gT[:, 0:8, :], ACT.Sigmoid).then_inc(S.gates_ready, 1)
            act.wait_ge(S.lnvar_ready, 1)
            f(rsb2, rsb2, ACT.Sqrt).then_inc(S.lnroot_ready, 1)
            act.wait_ge(S.lny_ready, 1)
            for j in range(CT):
                last = f(acc[:, j, :], acc[:, j, :], ACT.Silu, bias=par[:, R_LNB + j:R_LNB + j + 1],
                         scale=par[:, R_LNW + j:R_LNW + j + 1])
            last.then_inc(S.silu_ready, 1)
            for t in range(2):
                act.wait_ge(S.h1_ready, 2 * t + 2)
                f(xn[:, t, :], h1[:, t, :], ACT.Square, accum_out=ssh[:, t:t + 1]).then_inc(S.h1ss_ready, 1)
            act.wait_ge(S.h1var_ready, 1)
            f(rsh, ssh, ACT.Sqrt).then_inc(S.h1root_ready, 1)
            for t in range(2):
                for c in range(2):
                    nc.scalar.copy(xnT[:, 4 * c:4 * c + 4, t * P:(t + 1) * P],
                                   full(("xt", t, c)).rearrange("p (k n) -> p k n", k=4)).then_inc(S.xnT_ready, 1)
            f(lgT[0:E, :], full("lgt")[0:E, 0:SEQ], ACT.Identity, bias=rbc[0:E, :]).then_inc(S.lgT_ready, 1)
            act.wait_ge(S.top_ready, 1)
            e4 = tk[:, 0:8]
            f(e4, e4, ACT.Exp).then_inc(S.exp4_ready, 1)
            nc.scalar.copy(lgT[0:E, :], full("gt")[0:E, 0:SEQ]).then_inc(S.gateT_ready, 1)

            X, Y = psum[:, 6, :], psum[:, 7, :]

            def rows_out(n, i):
                act.wait_ge(S.gathered, n + 1)
                nc.scalar.copy(xe[i], X.rearrange("p (k s) -> p k s", k=KD)).then_inc(S.xe_ready, 1)

            def turned_out(n, i):
                act.wait_ge(S.turned, n + 1)
                nc.scalar.copy(sT[i], X.rearrange("p (j s) -> p j s", j=4)).then_inc(S.sT_ready, 1)

            def sigmoid(n):
                act.wait_ge(S.g_ready, n + 1)
                f(sg, g_s, ACT.Sigmoid, scale=ALPHA).then_inc(S.sg_ready, 1)

            def act_out(n):
                act.wait_ge(S.aT_done, n + 1)
                nc.scalar.copy(aT, Y.rearrange("p (c s) -> p c s", c=4)).then_inc(S.aT_ready, 1)

            def result_out(n):
                act.wait_ge(S.dn_done, 4 * n + 4)
                nc.scalar.copy(y_s, Y).then_inc(S.y_ready, 1)

            def item(n, i, final=False):
                if not final:
                    rows_out(n + 1, 1 - i)
                sigmoid(n)
                if not final:
                    turned_out(n + 1, 1 - i)
                act_out(n)
                result_out(n)

            rows_out(0, 0)
            turned_out(0, 0)
            item(0, 0)
            with act.Fori(0, E // 2 - 1) as it:
                item(2 * it + 1, 1)
                item(2 * it + 2, 0)
            item(E - 1, 1, final=True)
            act.wait_ge(S.overflow_ready, 1)
            count = act.value_load(ovni[0:1, :], min_val=0, max_val=EXTRA)
            with act.If(count > 0):
                with act.Fori(0, count) as j:
                    n = j + E
                    rows_out(n, 0)
                    turned_out(n, 0)
                    sigmoid(n)
                    act_out(n)
                    result_out(n)
            act.wait_ge(S.scattered, count + E)
            for i in range(2):
                nc.scalar.copy(ysb[:, i, :], psum[:, i, :]).then_inc(S.fin_act, 1)

        @block.vector
        def _(dve):
            chain = [0]
            tt, ts, stt = nc.vector.tensor_tensor, nc.vector.tensor_scalar, nc.vector.scalar_tensor_tensor

            def link(ins):
                chain[0] += 1
                ins.then_inc(dve_step, 1)
                dve.wait_ge(dve_step, chain[0])

            def full(job):
                bank, turn, _ = plan[job]
                dve.wait_ge(bank_full[bank], turn + 1)
                return psum[:, bank, :]

            for t in range(3):
                dve.wait_ge(S.xss_ready, t + 1)
                ts(ssx[:, t:t + 1], ssx[:, t:t + 1], 1.0 / D, EPS, ALU.mult, ALU.add).then_inc(S.xvar_ready, 1)
                dve.wait_ge(S.xroot_ready, t + 1)
                link(nc.vector.reciprocal(rsx[:, t:t + 1], rsx[:, t:t + 1]))
                r = TR[t]
                ts(xpos[0:r, t, :], xpos[0:r, t, :], rsx[0:r, t:t + 1], None, ALU.mult).then_inc(S.xs_ready, 1)
            dve.wait_ge(S.par_ready, 1)
            for t in range(3):
                r = TR[t]
                for c in range(2 if t < 2 else 1):
                    n = 4 if t < 2 else 8
                    b = full(("hn", t, c))[:, 0:n * r].rearrange("p (k j) -> p k j", k=n)
                    w = par[:, R_ATTN + 4 * c:R_ATTN + 4 * c + n].unsqueeze(2).to_broadcast([P, n, r])
                    tt(hnT[:, 4 * c:4 * c + n, t * P:t * P + r], b, w, ALU.mult).then_inc(S.hn_ready, 1)

            def conv_in(j):
                b = full(("ca", j))
                dve.wait_ge(S.csig_ready, j + 1)
                tt(hc[:, j, PAD:], b[:, 0:L], sig[:, j % 2, :], ALU.mult).then_inc(S.convin_ready, 1)

            taps = [(j, k) for j in range(CT) for k in range(TAPS)]
            tap = iter(taps)

            def conv_taps(n):
                for _ in range(n):
                    j, k = next(tap, (None, None))
                    if j is None:
                        return
                    w = dw[:, k * CT + j:k * CT + j + 1]
                    if k == 0:
                        ins = ts(acc[:, j, :], hc[:, j, 0:SEQ], w, par[:, R_DWB + j:R_DWB + j + 1], ALU.mult, ALU.add)
                    else:
                        ins = stt(acc[:, j, :], hc[:, j, k:k + SEQ], w, acc[:, j, :], ALU.mult, ALU.add)
                    if (j, k) == taps[-1]:
                        ins.then_inc(S.conv_ready, 1)
                    else:
                        link(ins)

            dve.wait_ge(S.pads_clear, 1)
            conv_in(0)
            ts(rsb, full("ssk")[:, 0:L], 1.0 / KVL, EPS, ALU.mult, ALU.add).then_inc(S.lvar_ready, 1)
            ts(rsb2, full("ssq")[:, 0:SEQ], 1.0 / QL, EPS, ALU.mult, ALU.add).then_inc(S.lvar_ready, 1)
            dve.wait_ge(S.lroot_ready, 1)
            link(nc.vector.reciprocal(rsb, rsb))
            stt(ckvn, ckvn, par[:, R_KVA:R_KVA + 1], rsb, ALU.mult, ALU.mult).then_inc(S.lat_ready, 1)
            dve.wait_ge(S.lroot_ready, 2)
            link(nc.vector.reciprocal(rsb2, rsb2))
            for j in range(2):
                last = stt(qnT[:, j, :], qnT[:, j, :], par[:, R_QA + j:R_QA + j + 1], rsb2, ALU.mult, ALU.mult)
            last.then_inc(S.lat_ready, 1)
            conv_in(1)
            conv_taps(24)
            conv_in(2)
            dve.wait_ge(in_cols, 80)

            def rotary(y, tiles, nr, rope, sq_ready):
                n, half = tiles * H, ROPE // 2
                heads = y.rearrange("p t (h d) -> p (t h) d", d=HD)
                weighted = tmp[:, 0:n * ROPE]
                link(tt(weighted.rearrange("p (g d) -> p g d", d=ROPE), heads[:, :, NOPE:HD],
                        nr.unsqueeze(1).to_broadcast([P, n, ROPE]), ALU.mult))
                w4 = weighted.rearrange("p (t h d) -> p t h d", t=tiles, h=H)
                y4 = y.rearrange("p t (h d) -> p t h d", d=HD)
                angles = const[:, rope:rope + ROPE * tiles].rearrange("p (t c) -> p t c", t=tiles)
                cos = angles[:, :, 0:half].unsqueeze(2).to_broadcast([P, tiles, H, half])
                sin = angles[:, :, half:ROPE].unsqueeze(2).to_broadcast([P, tiles, H, half])
                part = [tmp[:, (2 + i) * n * half:(3 + i) * n * half].rearrange("p (t h d) -> p t h d", t=tiles, h=H)
                        for i in range(4)]
                tt(part[0], w4[:, :, :, 0:half], cos, ALU.mult)
                tt(part[1], w4[:, :, :, half:ROPE], sin, ALU.mult)
                tt(part[2], w4[:, :, :, half:ROPE], cos, ALU.mult)
                link(tt(part[3], w4[:, :, :, 0:half], sin, ALU.mult))
                dve.wait_ge(sq_ready, 1)
                tt(y4[:, :, :, NOPE:NOPE + half], part[0], part[1], ALU.subtract)
                return tt(y4[:, :, :, NOPE + half:HD], part[2], part[3], ALU.add)

            def head_variance(ss, sq, ready):
                link(nc.vector.tensor_reduce(ss, sq.rearrange("p (g d) -> p g d", d=HD), AX_X, ALU.add))
                ts(ss, ss, 1.0 / HD, EPS, ALU.mult, ALU.add).then_inc(ready, 1)

            dve.wait_ge(S.kraw_ready, 1)
            link(rotary(kk, 3, knr, C_RK, S.ksq_ready))
            head_variance(hs, head_sq[0], S.khvar_ready)
            conv_taps(1)
            dve.wait_ge(S.khroot_ready, 1)
            link(nc.vector.reciprocal(hs, hs))
            k_heads = kk.rearrange("p t (h d) -> p (t h) d", d=HD)
            tt(k_heads, k_heads, hs.unsqueeze(2).to_broadcast([P, 3 * H, HD]), ALU.mult).then_inc(S.k_ready, 1)
            conv_in(3)
            dve.wait_ge(S.qraw_ready, 4)
            rotary(q, 2, qnr, C_RQ, S.qsq_ready).then_inc(S.q_ready, 1)
            head_variance(hsq, head_sq[1], S.qhvar_ready)
            for t in range(2):
                for c in range(2):
                    ts(qT[0:HD, 4 * c:4 * c + 4, t * P:(t + 1) * P],
                       full(("qt", t, c))[0:HD, :].rearrange("p (h j) -> p h j", h=4), qnc[0:HD, :], None,
                       ALU.mult).then_inc(S.qT_ready, 1)
            dve.wait_ge(S.qhroot_ready, 1)
            link(nc.vector.reciprocal(hsq, hsq))
            ts(qscale, hsq, SCALE, None, ALU.mult)
            link(ts(qnscale, hsq, -SCALE, None, ALU.mult))
            for s in range(2 * H):
                h, t = s // 2, s % 2
                b = full(("s", s))
                first = C_MASK + (P if t == 0 else 0)
                link(nc.vector.tensor_tensor_reduce(sm[:, t, 0:span(t)], b[:, 0:span(t)],
                                                    const[:, first:first + span(t)], 1.0, 4 * NEG, ALU.add, ALU.max,
                                                    mx[:, t:t + 1]))
                ts(nmx[:, t:t + 1], mx[:, t:t + 1], qnscale[:, t * H + h:t * H + h + 1], None, ALU.mult
                   ).then_inc(S.max_ready, 1)
                conv_taps(2)
                dve.wait_ge(S.exp_ready, s + 1)
                link(nc.vector.reciprocal(prs[:, t:t + 1], psm[:, t:t + 1]))
                ts(prob[:, t, 0:span(t)], prob[:, t, 0:span(t)], prs[:, t:t + 1], None, ALU.mult
                   ).then_inc(S.prob_ready, 1)
                conv_taps(4)
            conv_taps(len(taps))
            mean_sum = full("lnmu")[:, 0:SEQ].unsqueeze(1).to_broadcast([P, CT, SEQ])
            dve.wait_ge(S.conv_ready, 1)
            stt(acc, mean_sum, -1.0 / CONV, acc, ALU.mult, ALU.add).then_inc(S.lncent_ready, 1)

            def attention_mix(j):
                b = full(("ym", j)).rearrange("p (i n) -> p i n", i=2)
                dve.wait_ge(S.gates_ready, 1)
                tt(mixT[:, 2 * j:2 * j + 2, :], b, gT[:, 8 + 2 * j:10 + 2 * j, :], ALU.mult
                   ).then_inc(S.ymix_ready, 1)

            attention_mix(0)
            attention_mix(1)
            ts(rsb2, full("lnvar")[:, 0:SEQ], 1.0 / CONV, EPS, ALU.mult, ALU.add).then_inc(S.lnvar_ready, 1)
            dve.wait_ge(S.lnroot_ready, 1)
            link(nc.vector.reciprocal(rsb2, rsb2))
            tt(acc, acc, rsb2.unsqueeze(1).to_broadcast([P, CT, SEQ]), ALU.mult).then_inc(S.lny_ready, 1)
            attention_mix(2)
            attention_mix(3)
            dve.wait_ge(S.ymix_ready, 4)
            dve.wait_ge(S.gates_ready, 2)
            for j in range(4):
                b = full(("yc", j)).rearrange("p (i n) -> p i n", i=2)
                if j:
                    dve.wait_ge(S.mix_ready, j)
                link(tt(half_mix, b, gT[:, 2 * j:2 * j + 2, :], ALU.mult))
                tt(mixT[:, 2 * j:2 * j + 2, :], mixT[:, 2 * j:2 * j + 2, :], half_mix, ALU.add
                   ).then_inc(S.mix_ready, 1)
            dve.wait_ge(in_res, 32)
            for t in range(2):
                for c in range(2):
                    tt(h1[:, t, c * 512:(c + 1) * 512], full(("ho", t, c)), xres[:, t, c * 512:(c + 1) * 512],
                       ALU.add).then_inc(S.h1_ready, 1)
            dve.wait_ge(S.h1ss_ready, 2)
            ts(ssh, ssh, 1.0 / D, EPS, ALU.mult, ALU.add).then_inc(S.h1var_ready, 1)
            dve.wait_ge(S.h1root_ready, 1)
            link(nc.vector.reciprocal(rsh, rsh))
            dve.wait_ge(in_router, 32)
            for t in range(2):
                stt(xn[:, t, :], h1[:, t, :], rsh[:, t:t + 1], fnw, ALU.mult, ALU.mult).then_inc(S.xn_ready, 1)
            nc.vector.memset(biasgu, 0.0).then_inc(S.bias_clear, 1)
            nc.vector.memset(wp[0], 0.0)
            nc.vector.memset(wp[1], 0.0)
            for t in range(2):
                dve.wait_ge(S.hi_ready, t + 1)
                tt(rest[:, t, :], xn[:, t, :], xn3[:, t, 0, :], ALU.subtract).then_inc(S.rest_ready, 1)
            logits = tk[:, 8:72].rearrange("p (t e) -> p t e", t=2)
            link(nc.vector.tensor_copy(logits, full("lg")[:, 0:2 * E].rearrange("p (t e) -> p t e", t=2)))
            v8 = tk[:, 72:88].rearrange("p (t e) -> p t e", t=2)
            i8 = tk[:, 88:104].bitcast(U32).rearrange("p (t e) -> p t e", t=2)
            f8 = tk[:, 104:120].rearrange("p (t e) -> p t e", t=2)
            e4 = tk[:, 0:8].rearrange("p (t e) -> p t e", t=2)
            sum4, inv4 = tk[:, 120:122], tk[:, 122:124]
            hot = tk[:, 128:384].rearrange("p (t k e) -> p t k e", t=2, k=TOPK)
            for t in range(2):
                last = nc.vector.max(v8[:, t, :], logits[:, t, :])
            last.then_inc(S.logits_ready, 1)
            dve.wait_ge(S.logits_ready, 1)
            tt(e4, v8[:, :, 0:TOPK], v8[:, :, 0:1].to_broadcast([P, 2, TOPK]), ALU.subtract).then_inc(S.top_ready, 1)
            for t in range(2):
                link(nc.vector.max_index(i8[:, t, :], v8[:, t, :], logits[:, t, :]))
            link(nc.vector.tensor_copy(f8, i8))
            for t in range(2):
                last = tt(hot[:, t], iota[:, 0:E].unsqueeze(1).to_broadcast([P, TOPK, E]),
                          f8[:, t, 0:TOPK].unsqueeze(2).to_broadcast([P, TOPK, E]), ALU.is_equal)
            link(last)
            for t in range(2):
                last = nc.vector.tensor_reduce(maskt[:, t, :], hot[:, t].rearrange("p k e -> p e k"), AX_X, ALU.add)
            last.then_inc(S.mask_ready, 1)
            dve.wait_ge(S.exp4_ready, 1)
            link(nc.vector.tensor_reduce(sum4, e4, AX_X, ALU.add))
            link(nc.vector.reciprocal(inv4, sum4))
            link(tt(e4, e4, inv4.unsqueeze(2).to_broadcast([P, 2, TOPK]), ALU.mult))
            for t in range(2):
                last = tt(hot[:, t], hot[:, t], e4[:, t, :].unsqueeze(2).to_broadcast([P, TOPK, E]), ALU.mult)
            link(last)
            for t in range(2):
                last = nc.vector.tensor_reduce(gate[:, t, :], hot[:, t].rearrange("p k e -> p e k"), AX_X, ALU.add)
            last.then_inc(S.gate_ready, 1)
            dve.wait_ge(S.mask_ready, 1)
            link(stt(rankp, full("rank")[:, 0:2 * E].rearrange("p (t e) -> p t e", t=2), 1.0, maskt, ALU.add,
                     ALU.mult))
            ts(rankp, rankp, -1.0, None, ALU.add).then_inc(S.rank_ready, 1)
            counts = ov_s[:, 0:E]
            nc.vector.tensor_copy(counts, full("cnt")[:, 0:E]).then_inc(S.cnt_ready, 1)
            dve.wait_ge(S.rank_ready, 1)
            dve.wait_ge(S.gate_ready, 1)

            G, U = psum[:, 4, :], psum[:, 5, :]

            def build(e, i, base):
                numbers = iota[:, 0:SLOTS] if isinstance(base, int) else iota[:, bass.ds(base, SLOTS)]
                col = slice(e, e + 1) if isinstance(e, int) else bass.ds(e, 1)
                for t in range(2):
                    ts(ph[i][:, t, :], numbers, rankp[:, t, col], None, ALU.is_equal)
                    ts(wp[i][:, t, SLOTS:2 * SLOTS], numbers, rankp[:, t, col], gate[:, t, col], ALU.is_equal,
                       ALU.mult)
                nc.vector.tensor_copy(pick[i], ident[:, col].to_broadcast([P, SLOTS])).then_inc(S.built, 1)

            def activations(n):
                dve.wait_ge(S.gu_done, 8 * n + 8)
                ts(g_s, G, LIMIT, None, ALU.min).then_inc(S.g_ready, 1)
                ts(a_s, U, LIMIT, -LIMIT, ALU.min, ALU.max).then_inc(S.a_step, 1)
                dve.wait_ge(S.g_ready, n + 1)
                dve.wait_ge(S.a_step, 2 * n + 1)
                stt(a_s, a_s, 1.0, g_s, ALU.add, ALU.mult).then_inc(S.a_step, 1)
                dve.wait_ge(S.a_step, 2 * n + 2)
                dve.wait_ge(S.sg_ready, n + 1)
                tt(a_s, a_s, sg, ALU.mult).then_inc(S.act_ready, 1)

            build(0, 0, 0)
            for t in range(2):
                dve.wait_ge(S.mid_ready, t + 1)
                tt(xn3[:, t, 2, :], rest[:, t, :], xn3[:, t, 1, :], ALU.subtract).then_inc(S.split_ready, 1)
            build(1, 1, 0)
            valid, place = ov_s[:, 32:128], ov_s[:, 128:224]
            code = ov_s[:, 224:320]
            dve.wait_ge(S.cnt_ready, 1)
            for b in range(3):
                last = ts(valid[:, 32 * b:32 * b + 32], counts, float(SLOTS * (b + 1)), None, ALU.is_gt)
            link(last)
            nc.vector.tensor_tensor_scan(place, ones[:, 0:96], valid, 0.0, ALU.mult, ALU.add)
            tt(code, valid, iota[:, 0:96], ALU.mult)
            link(nc.vector.tensor_reduce(ovn, valid, AX_X, ALU.add))
            for j in range(EXTRA):
                link(stt(valid, place, float(j + 1), code, ALU.is_equal, ALU.mult, accum_out=ovf[:, j:j + 1]))
            turns1, turns2 = ov_s[:, 32:48], ov_s[:, 48:64]
            ts(turns1, ovf, 32.0, None, ALU.is_ge)
            link(ts(turns2, ovf, 64.0, None, ALU.is_ge))
            link(tt(turns1, turns1, turns2, ALU.add))
            link(ts(turns2, turns1, float(SLOTS), float(SLOTS), ALU.mult, ALU.add))
            link(stt(ovf, turns1, -32.0, ovf, ALU.mult, ALU.add))
            nc.vector.tensor_copy(ove, ovf)
            nc.vector.tensor_copy(ovb, turns2)
            nc.vector.tensor_copy(ovni, ovn).then_inc(S.overflow_ready, 1)
            activations(0)
            with dve.Fori(0, E // 2 - 1) as it:
                build(2 * it + 2, 0, 0)
                activations(2 * it + 1)
                build(2 * it + 3, 1, 0)
                activations(2 * it + 2)
            activations(E - 1)
            dve.wait_ge(S.overflow_ready, 1)
            count = dve.value_load(ovni[0:1, :], min_val=0, max_val=EXTRA)
            with dve.If(count > 0):
                with dve.Fori(0, count) as j:
                    e = dve.value_load(ove[0:1, bass.ds(j, 1)], min_val=0, max_val=E - 1)
                    base = dve.value_load(ovb[0:1, bass.ds(j, 1)], min_val=0, max_val=256 - SLOTS)
                    build(e, 0, base)
                    activations(j + E)
            dve.wait_ge(S.scattered, count + E)
            for i in range(2):
                nc.vector.tensor_copy(ysb[:, 2 + i, :], psum[:, 2 + i, :]).then_inc(S.fin_dve, 1)


_INS = ["x", "meta_tokens", "attn_norm_w", "w_in", "conv_dw_w", "conv_dw_b", "conv_ln_w", "conv_ln_b", "conv_pw2_w",
        "q_a_norm_w", "w_q_b", "kv_a_norm_w", "w_kv_b", "q_norm_w", "k_norm_w", "w_o_mla", "gate_b", "w_out",
        "ffn_norm_w", "router_w", "router_b", "w_gate_up", "b_gate_up", "w_down", "b_down"]


def kernel(**inputs):
    import concourse.bacc as bacc
    from concourse.bass_utils import run_bass_kernel_spmd

    nc = bacc.Bacc("TRN2", target_bir_lowering=False, num_devices=1)
    arrays = {f"in_{name}": np.ascontiguousarray(inputs[name]) for name in _INS}
    arrays["in_const"] = constants()
    args = {name[3:]: nc.dram_tensor(name, v.shape, mybir.dt.from_np(v.dtype), kind="ExternalInput").ap()
            for name, v in arrays.items()}
    out = nc.dram_tensor("out_y", (1, SEQ, D), F32, kind="ExternalOutput").ap()
    layer(nc, args, out)
    r = run_bass_kernel_spmd(nc, [arrays], core_ids=[0])
    return r.results[0]["out_y"]
```

```python
from contextlib import ExitStack

import numpy as np

import concourse.bass as bass
from concourse import mybir

F32 = mybir.dt.float32
BF16 = mybir.dt.bfloat16
I32 = mybir.dt.int32
U32 = mybir.dt.uint32
ALU = mybir.AluOpType
ACT = mybir.ActivationFunctionType
AX_X = mybir.AxisListType.X

P = 128
D = 1024
KD = D // P
SEQ = 256
META = 16
L = SEQ + META
CONV = 512
CT = CONV // P
TAPS = 31
PAD = TAPS - 1 - META
H = 8
NOPE, ROPE, VD = 64, 32, 64
HD = NOPE + ROPE
QL = 256
KVL = 128
COL_Q = 2 * CONV
COL_KV = COL_Q + QL
COL_G = COL_KV + KVL + ROPE
E = 32
TOPK = 4
FF = 1024
SLOTS = 64
EXTRA = SEQ * TOPK // SLOTS
LIMIT, ALPHA = 7.0, 1.702
EPS = 1e-6
NEG = -1e30
SCALE = float(HD) ** -0.5

C_ID, C_ONE, C_TRI, C_MASK, C_IOTA, C_RK, C_RQ, C_END = 0, 128, 256, 384, 656, 912, 1008, 1072
R_ATTN, R_DWB, R_LNW, R_LNB, R_QA, R_KVA, R_GB, R_FFN, R_END = 0, 8, 12, 16, 20, 22, 23, 39, 47


def constants():
    c = np.zeros((P, C_END), np.float32)
    c[:, C_ID:C_ID + P] = np.eye(P)
    c[:, C_ONE:C_ONE + P] = 1.0
    c[:, C_TRI:C_TRI + P] = np.triu(np.ones((P, P)), 1)
    c[:, C_MASK + 144:C_MASK + 272] = np.triu(np.full((P, P), NEG), 1)
    c[:, C_IOTA:C_IOTA + 256] = np.arange(256)
    half = ROPE // 2
    inv = np.float32(10000.0) ** (-np.arange(half, dtype=np.float32) / np.float32(half))
    for col, first in [(C_RK, 0), (C_RK + 32, 128), (C_RK + 64, 256), (C_RQ, META), (C_RQ + 32, META + 128)]:
        ang = (first + np.arange(P)).astype(np.float32)[:, None] * inv[None, :].astype(np.float32)
        c[:, col:col + half] = np.cos(ang)
        c[:, col + half:col + 2 * half] = np.sin(ang)
    return c


def bank_plan():
    plan, turns = {}, [[] for _ in range(8)]

    def add(job, bank, release, value):
        plan[job] = (bank, len(turns[bank]), (release, value))
        turns[bank].append(job)

    add("par", 0, "par_ready", 1)
    for i, job in enumerate([("hn", 0, 0), ("hn", 0, 1), ("hn", 1, 0), ("hn", 1, 1), ("hn", 2, 0)]):
        add(job, 1 + i, "hn_ready", i + 1)
    order = [("ckv", "squares", 1), ("kpe", "kpe_ready", 1), ("q", "squares", 2)]
    conv = lambda j: [(("ca", j), "convin_ready", j + 1), (("cg", j), "csig_ready", j + 1)]
    order += conv(0) + [("ssk", "lvar_ready", 1), ("ssq", "lvar_ready", 2)] + conv(1)
    order += [(("kvb", t, c), "v_ready", 2 * t + c + 1) for t in range(3) for c in range(2)]
    order += [("kpet", "kraw_ready", 1)] + conv(2)
    order += [(("qb", t, c), "qraw_ready", 2 * t + c + 1) for t in range(2) for c in range(2)] + conv(3)
    order += [(("kt", t, c), "kT_ready", 2 * t + c + 1) for t in range(3) for c in range(2 if t < 2 else 1)]
    order += [(("qt", t, c), "qT_ready", 2 * t + c + 1) for t in range(2) for c in range(2)]
    for i, (job, release, value) in enumerate(order):
        add(job, (6 + i) % 8, release, value)
    for s in range(2 * H):
        add(("gate", s), 2 + s % 2, "gT_ready", s + 1)
        add(("s", s), 4 + s % 2, "max_ready", s + 1)
        add(("pt", s), 6 + s % 2, "probT_ready", s + 1)
        if s % 4 == 0:
            add(("ot", s // 4), s // 4 % 2, "oT_ready", s // 4 + 1)
    add("lnmu", 6, "lncent_ready", 1)
    for j in range(2):
        add(("ym", j), 4 + j, "ymix_ready", j + 1)
    add("lnvar", 7, "lnvar_ready", 1)
    for j in range(2, 4):
        add(("ym", j), [6, 4][j - 2], "ymix_ready", j + 1)
    for j in range(4):
        add(("yc", j), [5, 7, 6, 4][j], "mix_ready", j + 1)
    for t in range(2):
        for c in range(2):
            add(("ho", t, c), 2 * t + c, "h1_ready", 2 * t + c + 1)
    for t in range(2):
        for c in range(2):
            add(("ht", t, c), [5, 7, 7, 5][2 * t + c], "hT_ready", 2 * t + c + 1)
        add(("lg", t), [5, 7][t], "logits_ready", t + 1)
        if t == 0:
            add("rank", 6, "rank_ready", 1)
            add("cnt", 4, "cnt_ready", 1)
    add("gt", 5, "gateT_ready", 1)
    return plan, turns


def layer(nc, a, out):
    plan, turns = bank_plan()
    ctx = ExitStack()
    with ctx:
        named = {}

        def sem(name):
            named[name] = ctx.enter_context(nc.semaphore(name))
            return named[name]

        GU, DN, W = 16384, 8192, 12248
        arena = ctx.enter_context(nc.sbuf_tensor("arena", [P, 2 * GU + DN + W], F32))
        psum = ctx.enter_context(nc.psum_tensor("psum", [P, 8, 512], F32))

        def words(at, n):
            return arena[:, at:at + n]

        def grid(at, x, y):
            return words(at, x * y).rearrange("p (x y) -> p x y", x=x)

        A0, B0, D0, W0 = 0, GU, 2 * GU, 2 * GU + DN
        gu = [[words((A0, B0)[i] + 2048 * k, 2048) for k in range(KD)] for i in range(2)]
        dn = [grid(D0 + 2048 * i, 2, 1024) for i in range(4)]

        RING = 6
        win = [grid(A0 + 2048 * s, KD, 256) for s in range(RING)]
        at = A0 + 2048 * RING
        hnT = grid(at, KD, L); at += KD * L
        qnT = grid(at, 2, SEQ); at += 2 * SEQ
        ckvn = words(at, L); at += L
        sqq = grid(at, 2, SEQ); at += 2 * SEQ
        sqk = words(at, L); at += L
        kpeT = words(at, L)
        wo = grid(D0, 4, D)
        pw2 = grid(D0 + 4096, 4, D)
        xpos = grid(B0, 3, D)
        junk = words(B0 + 4096, D)
        head_sq = [words(B0, 3 * H * HD), words(B0 + 3 * H * HD, 2 * H * HD)]
        gT = grid(B0, 16, SEQ)
        mixT = grid(B0 + 4096, KD, SEQ)
        hc = grid(B0 + 6144, CT, PAD + L)
        sqc = grid(B0 + 6144, CT, SEQ)
        half_mix = grid(B0 + 6144, 2, SEQ)
        rsb = words(B0 + 7296, L)
        rsb2 = words(B0 + 7296 + L, SEQ)
        h1 = grid(B0, 2, D)
        xn = grid(B0 + 2048, 2, D)
        rest = words(B0 + 6144, D)
        hT = [grid(B0 + 7168, KD, P), grid(B0 + 4096, KD, P)]
        at = B0 + 8192
        q = grid(at, 2, H * HD); at += 2 * H * HD
        kk = grid(at, 3, H * HD); at += 3 * H * HD
        v = grid(at, 3, H * VD); at += 3 * H * VD
        wqb = grid(at, 2, H * HD); at += 2 * H * HD
        wkvb = words(at, H * 128)
        rows = grid(B0 + 8192, 2, P)
        wout = grid(B0 + 8192, KD, D)
        const = words(W0, C_END)
        at = W0 + C_END
        par = words(at, R_END); at += R_END
        dw = words(at, TAPS * CT); at += TAPS * CT
        small = words(at, 384); at += 384
        WB = at
        acc = grid(at, CT, SEQ); at += CT * SEQ
        xres = [words(at, D), words(W0 + W - D, D)]
        qT = grid(at, H, SEQ); at += H * SEQ
        kT = grid(at, H, L); at += H * L
        oT = grid(at, 4, SEQ); at += 4 * SEQ
        sig = grid(at, 2, L); at += 2 * L
        tmp = words(at, 2304)
        prob = grid(at, 2, L)
        probT = grid(at + 2 * L, 2, 384)
        sm = grid(at + 2 * L + 768, 2, L); at += 2304
        assert at <= W0 + W - D
        at = WB
        xn3 = words(at, 3072).bitcast(BF16).rearrange("p (t s d) -> p t s d", t=2, s=3); at += 3072
        biasgu = words(at, 2 * FF); at += 2 * FF
        wp = [grid(at + 384 * i, 2, 192) for i in range(2)]; at += 768
        ph = [words(at + 64 * i, 64).bitcast(BF16).rearrange("p (t s) -> p t s", t=2) for i in range(2)]; at += 128
        pick = [words(at + 64 * i, 64) for i in range(2)]; at += 128
        xe = [grid(at + 1024 * i, KD, SLOTS) for i in range(2)]
        sT = [grid(at + 1024 * i + 512, 4, P) for i in range(2)]
        bdown = words(at + 1024, D); at += 2048
        fnw = words(at, D)
        rwt = grid(at + D, KD, E)
        tk = words(at + D + 512, 512)
        router_bias = tk[:, 384:384 + E]
        gateT = tk[:, 128:384]
        g_s = words(at, 512); at += 512
        sg = words(at, 512)
        aT = grid(at, 4, P); at += 512
        a_s = words(at, 512); at += 512
        y_s = words(at, 512); at += 512
        assert at <= W0 + W
        ov_s = words(at, 320)
        assert at + 320 <= W0 + W
        ysb = grid(A0, 4, 512)

        ident, ones = const[:, C_ID:C_ID + P], const[:, C_ONE:C_ONE + P]
        tri, iota = const[:, C_TRI:C_TRI + P], const[:, C_IOTA:C_IOTA + 256]

        def cols(i, n):
            return small[:, i:i + n]

        ssx, rsx, knc, qnc, knr, qnr, hs = cols(0, 3), cols(3, 3), cols(6, 1), cols(7, 1), cols(8, 32), cols(40, 32), \
            cols(72, 24)
        mx, nmx, psm, prs = cols(96, 2), cols(98, 2), cols(100, 2), cols(102, 2)
        ssh, rsh, ovn = cols(105, 2), cols(107, 2), cols(109, 1)
        ovni = cols(110, 1).bitcast(I32)
        hsq, warm, tables = cols(111, 16), cols(127, 1), cols(368, 16)
        qscale, qnscale = cols(320, 16), cols(336, 16)
        rankp, gate, maskt = (cols(i, 64).rearrange("p (t e) -> p t e", t=2) for i in (128, 192, 256))
        ovf = cols(320, 16)
        ove, ovb = cols(336, 16).bitcast(I32), cols(352, 16).bitcast(I32)

        bank_full = [sem(f"bank_full{b}") for b in range(8)]
        dve_step, act_step, pool_step = sem("dve_step"), sem("act_step"), sem("pool_step")
        in_const, in_rows, in_cols = sem("in_const"), sem("in_rows"), sem("in_cols")
        in_x = [sem(f"in_x{t}") for t in range(3)]
        in_win = [sem(f"in_win{s}") for s in range(RING)]
        in_wqb, in_wkvb, in_wo, in_pw2 = sem("in_wqb"), sem("in_wkvb"), sem("in_wo"), sem("in_pw2")
        in_wout, in_res, in_router, in_bias = sem("in_wout"), sem("in_res"), sem("in_router"), sem("in_bias")
        in_gu = [[sem(f"in_gu{i}_{k}") for k in range(KD)] for i in range(2)]
        in_dn = [sem(f"in_dn{i}") for i in range(4)]
        for name in ("cols_clear pads_clear bias_clear par_ready xss_ready xvar_ready xroot_ready xs_ready hn_ready "
                     "squares kpe_ready lvar_ready lroot_ready lat_ready csig_ready convin_ready v_ready "
                     "kraw_ready qraw_ready ksq_ready qsq_ready khvar_ready khroot_ready qhvar_ready qhroot_ready k_ready q_ready "
                     "kT_ready qT_ready max_ready exp_ready prob_ready probT_ready gT_ready gates_ready oT_ready conv_ready "
                     "lncent_ready lnsq_ready lnvar_ready lnroot_ready lny_ready silu_ready ymix_ready mix_ready "
                     "h1_ready h1ss_ready h1var_ready h1root_ready xn_ready hT_ready hi_ready rest_ready pick_clear "
                     "mid_ready split_ready wout_used router_ready logits_ready top_ready exp4_ready mask_ready rank_ready "
                     "cnt_ready gate_ready gateT_ready overflow_ready gu_done dn_done built gathered "
                     "xe_ready turned sT_ready g_ready a_step sg_ready act_ready aT_done aT_ready y_ready scattered "
                     "fin_act fin_dve stored").split():
            sem(name)
        S = type("Semaphores", (), named)

        block = ctx.enter_context(nc.Block())

        TR = [P, P, META]
        pieces = ["kv", "q"] + [("c", j) for j in range(CT)] + [("g", j) for j in range(8)]
        piece_at = {name: (i % RING, 32 * (i // RING + 1)) for i, name in enumerate(pieces)}
        piece_used = {"kv": (S.kpe_ready, 1), "q": (S.squares, 2)}
        piece_used.update({("c", j): (S.csig_ready, j + 1) for j in range(CT)})
        piece_used.update({("g", j): (S.gT_ready, 2 * j + 2) for j in range(8)})
        w_in, x = a["w_in"][0], a["x"][0]
        weights_gu, weights_dn = a["w_gate_up"][0], a["w_down"][0]

        def span(t):
            return META + P * (t + 1)

        @block.sync
        def _(sp):
            sp.dma_start(xpos[0:META, 0, :], a["meta_tokens"]).then_inc(in_x[0], 16)
            sp.dma_start(xpos[META:P, 0, :], x[0:P - META, :]).then_inc(in_x[0], 16)
            sp.dma_start(xpos[:, 1, :], x[P - META:2 * P - META, :]).then_inc(in_x[1], 16)
            sp.dma_start(xpos[0:META, 2, :], x[2 * P - META:SEQ, :]).then_inc(in_x[2], 16)
            sp.dma_start(const, a["const"]).then_inc(in_const, 16)

            def load_win(i):
                slot, name = i % RING, pieces[i]
                if i >= RING:
                    sp.wait_ge(*piece_used[pieces[i - RING]])
                src = w_in.rearrange("(k p) c -> p k c", p=P)
                if name == "kv":
                    parts = [(0, COL_KV, KVL), (KVL, COL_KV + KVL, ROPE)]
                elif name == "q":
                    parts = [(0, COL_Q, P), (P, COL_Q + P, P)]
                elif name[0] == "c":
                    parts = [(0, P * name[1], P), (P, CONV + P * name[1], P)]
                else:
                    parts = [(0, COL_G + 256 * name[1], P), (P, COL_G + 256 * name[1] + P, P)]
                for to, frm, n in parts:
                    sp.dma_start(win[slot][:, :, to:to + n], src[:, :, frm:frm + n]).then_inc(in_win[slot], 16)

            load_win(0)
            for src, row, n in [("attn_norm_w", R_ATTN, 8), ("conv_dw_b", R_DWB, 4), ("conv_ln_w", R_LNW, 4),
                                ("conv_ln_b", R_LNB, 4), ("q_a_norm_w", R_QA, 2), ("kv_a_norm_w", R_KVA, 1),
                                ("gate_b", R_GB, 16), ("ffn_norm_w", R_FFN, 8)]:
                sp.dma_start(rows[row:row + n, 0, :], a[src][0].rearrange("(r c) -> r c", c=P)
                            ).then_inc(in_rows, 16)
            sp.dma_start(rows[0:TAPS * CT, 1, :], a["conv_dw_w"][0].rearrange("j (c p) -> (j c) p", p=P)
                         ).then_inc(in_rows, 16)
            for i in range(1, 4):
                load_win(i)
            sp.wait_ge(S.par_ready, 1)
            sp.dma_start(wkvb, a["w_kv_b"][0]).then_inc(in_wkvb, 16)
            sp.dma_start(wqb, a["w_q_b"][0].rearrange("(k p) c -> p k c", p=P)).then_inc(in_wqb, 16)
            for i in range(4, 10):
                load_win(i)
            sp.dma_start(wo, a["w_o_mla"][0].rearrange("(k p) c -> p k c", p=P)).then_inc(in_wo, 16)
            sp.dma_start(pw2, a["conv_pw2_w"][0].rearrange("(k p) c -> p k c", p=P)).then_inc(in_pw2, 16)
            sp.dma_start(xres[1], x[P:2 * P, :]).then_inc(in_res, 16)
            for i in range(10, len(pieces)):
                load_win(i)

            def load_gu(e, i, k):
                if isinstance(e, int):
                    src = weights_gu[e, k * P:(k + 1) * P, :]
                else:
                    src = weights_gu[bass.ds(e, 1), k * P:(k + 1) * P, :].rearrange("a p c -> (a p) c")
                sp.dma_start(gu[i][k], src).then_inc(in_gu[i][k], 16)

            def load_dn(e, i):
                src = weights_dn[e:e + 1] if isinstance(e, int) else weights_dn[bass.ds(e, 1)]
                src = src[:, 2 * i * P:(2 * i + 2) * P, :].rearrange("a (k p) c -> p (a k) c", p=P)
                sp.dma_start(dn[i], src).then_inc(in_dn[i], 16)

            for k in range(2, 6):
                sp.wait_ge(*piece_used["g", k])
                load_gu(0, 0, k)
            sp.wait_ge(S.oT_ready, 4)
            sp.dma_start(xres[0], x[0:P, :]).then_inc(in_res, 16)
            sp.dma_start(wout, a["w_out"][0].rearrange("(k p) c -> p k c", p=P)).then_inc(in_wout, 16)
            sp.dma_start(fnw, a["ffn_norm_w"][0].partition_broadcast(P)
                         ).then_inc(in_router, 16)
            sp.dma_start(rwt, a["router_w"][0].rearrange("(k p) e -> p k e", p=P)).then_inc(in_router, 16)
            sp.dma_start(router_bias, a["router_b"][0].partition_broadcast(P)).then_inc(in_router, 16)
            for k in (0, 1, 6, 7):
                load_gu(0, 0, k)
            sp.wait_ge(S.mix_ready, 4)
            for i in range(4):
                load_dn(0, i)
            for k in range(4, 8):
                if k < 7:
                    sp.wait_ge(S.wout_used, k - 3)
                else:
                    sp.wait_ge(S.h1_ready, 4)
                load_gu(1, 1, k)
            sp.wait_ge(S.xn_ready, 2)
            sp.wait_ge(S.hT_ready, 4)
            load_gu(1, 1, 0)
            sp.wait_ge(S.logits_ready, 2)
            load_gu(1, 1, 2)
            sp.wait_ge(S.split_ready, 2)
            for k in (1, 3):
                load_gu(1, 1, k)
            def next_gu(n, u):
                for k in range(KD):
                    sp.wait_ge(S.gu_done, 8 * (n - 2) + (k + 1))
                    load_gu(n, u, k)

            def next_dn(n):
                for i in range(4):
                    sp.wait_ge(S.dn_done, 4 * (n - 1) + (i + 1))
                    load_dn(n, i)

            EARLY = 6
            with sp.Fori(0, EARLY // 2) as it:
                for u in range(2):
                    next_gu(2 * it + (2 + u), u)
                    next_dn(2 * it + (1 + u))
            next_dn(EARLY + 1)
            with sp.Fori(0, (E - EARLY - 2) // 2) as it:
                for u in range(2):
                    next_gu(2 * it + (EARLY + 2 + u), u)
                    next_dn(2 * it + (EARLY + 2 + u))
            sp.wait_ge(S.overflow_ready, 1)
            count = sp.value_load(ovni[0:1, :], min_val=0, max_val=EXTRA)
            with sp.If(count > 0):
                with sp.Fori(0, count) as j:
                    e = sp.value_load(ove[0:1, bass.ds(j, 1)], min_val=0, max_val=E - 1)
                    sp.wait_ge(S.gu_done, 8 * j + 8 * E)
                    for k in range(KD):
                        load_gu(e, 0, k)
                    sp.wait_ge(S.dn_done, 4 * j + 4 * E)
                    for i in range(4):
                        load_dn(e, i)
            for i in range(4):
                sp.wait_ge(S.fin_act if i < 2 else S.fin_dve, i % 2 + 1)
                sp.dma_start(out[0, (i // 2) * P:(i // 2 + 1) * P, (i % 2) * 512:(i % 2 + 1) * 512], ysb[:, i, :]
                             ).then_inc(S.stored, 16)
            sp.wait_ge(S.stored, 64)

        @block.gpsimd
        def _(pool):
            nc.gpsimd.memset(small, 1.0).then_inc(S.cols_clear, 1)
            pool.wait_ge(S.cols_clear, 1)
            with nc.allow_non_contiguous_dma(reason="one value a partition"):
                for to, src in [(knc, "k_norm_w"), (qnc, "q_norm_w")]:
                    pool.dma_start(to[0:NOPE, :], a[src][0, 0:NOPE].rearrange("(p a) -> p a", a=1)
                                   ).then_inc(in_cols, 16)
            for to, src in [(knr, "k_norm_w"), (qnr, "q_norm_w")]:
                pool.dma_start(to, a[src][0, NOPE:HD].partition_broadcast(P)
                               ).then_inc(in_cols, 16)
            nc.gpsimd.memset(hc[:, :, 0:PAD], 0.0).then_inc(S.pads_clear, 1)
            pool.wait_ge(S.par_ready, 1)
            nc.gpsimd.memset(kk[:, 2, :], 0.0).then_inc(S.pads_clear, 1)
            pool.wait_ge(S.oT_ready, 4)
            nc.gpsimd.memset(biasgu, 0.0).then_inc(S.bias_clear, 1)
            pool.wait_ge(S.bias_clear, 1)
            pool.dma_start(biasgu[0:E, :], a["b_gate_up"][0]).then_inc(in_bias, 16)
            pool.wait_ge(S.ymix_ready, 4)
            for i in range(2):
                nc.gpsimd.memset(wp[i], 0.0).then_inc(S.pick_clear, 1)
            pool.dma_start(bdown[0:E, :], a["b_down"][0]).then_inc(in_bias, 16)

        @block.tensor
        def _(pe):
            mm = nc.tensor.matmul

            def fill(job):
                bank, turn, _ = plan[job]
                if turn:
                    release, value = plan[turns[bank][turn - 1]][2]
                    pe.wait_ge(named[release], value)
                return psum[:, bank, :]

            def filled(job, ins):
                ins.then_inc(bank_full[plan[job][0]], 1)

            pe.wait_ge(in_const, 16)
            pe.wait_ge(in_rows, 16 * 9)
            b = fill("par")
            nc.tensor.transpose(b[:, 0:R_END], rows[0:R_END, 0, :], ident[0:R_END, 0:R_END])
            filled("par", nc.tensor.transpose(b[:, 128:128 + TAPS * CT], rows[0:TAPS * CT, 1, :],
                                              ident[0:TAPS * CT, 0:TAPS * CT]))
            for t in range(3):
                pe.wait_ge(S.xs_ready, t + 1)
                r = TR[t]
                for c in range(2 if t < 2 else 1):
                    b = fill(("hn", t, c))
                    for k in range(4 if t < 2 else 8):
                        kt = 4 * c + k
                        last = nc.tensor.transpose(b[:, r * k:r * (k + 1)], xpos[0:r, t, kt * P:(kt + 1) * P],
                                                   ident[0:r, 0:r])
                    filled(("hn", t, c), last)
            pe.wait_ge(S.hn_ready, 5)

            def project(b, piece, c0, m, n0, n):
                slot, value = piece_at[piece]
                pe.wait_ge(in_win[slot], value)
                for k in range(KD):
                    last = mm(b, win[slot][:, k, c0:c0 + m], hnT[:, k, n0:n0 + n], start=(k == 0),
                              stop=(k == KD - 1))
                return last

            filled("ckv", project(fill("ckv")[:, 0:L], "kv", 0, P, 0, L))
            filled("kpe", project(fill("kpe")[0:ROPE, 0:L], "kv", P, ROPE, 0, L))
            b = fill("q")
            for j in range(2):
                last = project(b[:, j * SEQ:(j + 1) * SEQ], "q", P * j, P, META, SEQ)
            filled("q", last)

            def conv_tile(j):
                filled(("ca", j), project(fill(("ca", j))[:, 0:L], ("c", j), 0, P, 0, L))
                filled(("cg", j), project(fill(("cg", j))[:, 0:L], ("c", j), P, P, 0, L))

            conv_tile(0)
            pe.wait_ge(S.squares, 1)
            filled("ssk", mm(fill("ssk")[:, 0:L], ones, sqk, start=True, stop=True))
            pe.wait_ge(S.squares, 2)
            b = fill("ssq")[:, 0:SEQ]
            for j in range(2):
                last = mm(b, ones, sqq[:, j, :], start=(j == 0), stop=(j == 1))
            filled("ssq", last)
            conv_tile(1)
            pe.wait_ge(in_wkvb, 16)
            pe.wait_ge(S.lat_ready, 1)
            for t in range(3):
                for c in range(2):
                    filled(("kvb", t, c), mm(fill(("kvb", t, c))[0:TR[t], :], ckvn[:, t * P:t * P + TR[t]],
                                             wkvb[:, c * 512:(c + 1) * 512], start=True, stop=True))
            pe.wait_ge(S.kpe_ready, 1)
            b = fill("kpet")
            for t in range(3):
                last = nc.tensor.transpose(b[0:TR[t], t * ROPE:(t + 1) * ROPE], kpeT[0:ROPE, t * P:t * P + TR[t]],
                                           ident[0:ROPE, 0:ROPE])
            filled("kpet", last)
            conv_tile(2)
            pe.wait_ge(in_wqb, 16)
            pe.wait_ge(S.lat_ready, 2)
            for t in range(2):
                for c in range(2):
                    b = fill(("qb", t, c))[:, 0:384]
                    for k in range(2):
                        last = mm(b, qnT[:, k, t * P:(t + 1) * P], wqb[:, k, c * 384:(c + 1) * 384],
                                  start=(k == 0), stop=(k == 1))
                    filled(("qb", t, c), last)
            conv_tile(3)
            pe.wait_ge(S.k_ready, 1)
            for t in range(3):
                r = TR[t]
                for c in range(2 if t < 2 else 1):
                    b = fill(("kt", t, c))
                    for i in range(4 if t < 2 else 8):
                        h = 4 * c + i
                        last = nc.tensor.transpose(b[0:HD, r * i:r * (i + 1)], kk[0:r, t, h * HD:(h + 1) * HD],
                                                   ident[0:r, 0:r])
                    filled(("kt", t, c), last)
            pe.wait_ge(S.q_ready, 1)
            for t in range(2):
                for c in range(2):
                    b = fill(("qt", t, c))
                    for i in range(4):
                        h = 4 * c + i
                        last = nc.tensor.transpose(b[0:HD, P * i:P * (i + 1)], q[:, t, h * HD:(h + 1) * HD], ident)
                    filled(("qt", t, c), last)

            def scores(s):
                h, t = s // 2, s % 2
                filled(("s", s), mm(fill(("s", s))[:, 0:span(t)], qT[0:HD, h, t * P:(t + 1) * P],
                                    kT[0:HD, h, 0:span(t)], start=True, stop=True))

            def gate_tile(s, first, last):
                b = fill(("gate", s)) if first == 0 else psum[:, plan["gate", s][0], :]
                slot, value = piece_at["g", s // 2]
                pe.wait_ge(in_win[slot], value)
                for k in range(first, last):
                    ins = mm(b[:, 0:SEQ], win[slot][:, k, P * (s % 2):P * (s % 2) + P], hnT[:, k, META:META + SEQ],
                             start=(k == 0), stop=(k == KD - 1))
                if last == KD:
                    filled(("gate", s), ins)

            def residual(t):
                pe.wait_ge(in_res, 32 - 16 * t)
                for c in range(2):
                    mm(fill(("ho", t, c)), ident, xres[t][:, c * 512:(c + 1) * 512], start=True, stop=False,
                       skip_group_check=True)

            gate_tile(0, 0, KD)
            pe.wait_ge(S.kT_ready, 5)
            pe.wait_ge(S.qT_ready, 4)
            scores(0)

            def values(s):
                h, t = s // 2, s % 2
                if s % 4 == 0:
                    fill(("ot", s // 4))
                b = psum[64 * (h % 2):64 * (h % 2) + VD, plan[("ot", s // 4)][0], t * P:(t + 1) * P]
                pe.wait_ge(S.probT_ready, s + 1)
                tiles = key_tiles(t)
                for i, (c0, n) in enumerate(tiles):
                    last = mm(b, v[0:n, c0 // P, h * VD:(h + 1) * VD], probT[0:n, s % 2, i * P:(i + 1) * P],
                              start=(i == 0), stop=(i == len(tiles) - 1))
                if s % 4 == 3:
                    filled(("ot", s // 4), last)

            def key_tiles(t):
                return [(c0, min(P, span(t) - c0)) for c0 in range(0, span(t), P)]

            for s in range(2 * H):
                if s + 1 < 2 * H:
                    gate_tile(s + 1, 0, 2)
                if s:
                    values(s - 1)
                if s + 1 < 2 * H:
                    gate_tile(s + 1, 2, KD)
                else:
                    residual(1)
                pe.wait_ge(S.prob_ready, s + 1)
                b = fill(("pt", s))
                for i, (c0, n) in enumerate(key_tiles(s % 2)):
                    last = nc.tensor.transpose(b[0:n, i * P:(i + 1) * P], prob[:, s % 2, c0:c0 + n], ident)
                filled(("pt", s), last)
                if s + 1 < 2 * H:
                    scores(s + 1)
            values(2 * H - 1)
            def mixer(job, w, act_t):
                b = fill(job)
                for i in range(2):
                    m = 2 * job[1] + i
                    for k in range(4):
                        last = mm(b[:, i * SEQ:(i + 1) * SEQ], w[:, k, m * P:(m + 1) * P], act_t[:, k, :],
                                  start=(k == 0), stop=(k == 3))
                filled(job, last)

            pe.wait_ge(in_wo, 16)
            pe.wait_ge(S.oT_ready, 4)
            mixer(("ym", 0), wo, oT)
            pe.wait_ge(S.conv_ready, 1)
            b = fill("lnmu")[:, 0:SEQ]
            for j in range(CT):
                last = mm(b, ones, acc[:, j, :], start=(j == 0), stop=(j == CT - 1))
            filled("lnmu", last)
            for j in range(1, 4):
                if j == 2:
                    pe.wait_ge(S.lnsq_ready, 1)
                    b = fill("lnvar")[:, 0:SEQ]
                    for c in range(CT):
                        last = mm(b, ones, sqc[:, c, :], start=(c == 0), stop=(c == CT - 1))
                    filled("lnvar", last)
                mixer(("ym", j), wo, oT)
            residual(0)
            pe.wait_ge(in_pw2, 16)
            pe.wait_ge(S.silu_ready, 1)
            for j in range(4):
                mixer(("yc", j), pw2, acc)
            pe.wait_ge(in_wout, 16)

            def total(t, c):
                return psum[:, 2 * t + c, :]

            def project_out(t, first, last):
                for k in range(first, last):
                    pe.wait_ge(S.mix_ready, k // 2 + 1)
                    for c in range(2):
                        ins = mm(total(t, c), mixT[:, k, t * P:(t + 1) * P], wout[:, k, c * 512:(c + 1) * 512],
                                 start=False, stop=False, skip_group_check=True)
                        if k == KD - 1:
                            filled(("ho", t, c), ins)
                    if t == 1 and k in (1, 3, 5):
                        ins.then_inc(S.wout_used, 1)

            def turn_state(t):
                for c in range(2):
                    pe.wait_ge(S.h1_ready, 2 * t + c + 1)
                    b = fill(("ht", t, c))
                    for k in range(4):
                        kt = 4 * c + k
                        last = nc.tensor.transpose(b[:, k * P:(k + 1) * P], h1[:, t, kt * P:(kt + 1) * P], ident)
                    filled(("ht", t, c), last)

            def router(t):
                pe.wait_ge(S.router_ready, 1)
                b = fill(("lg", t))[:, 0:E]
                for k in range(KD):
                    if k % 4 == 0:
                        pe.wait_ge(S.hT_ready, 2 * t + k // 4 + 1)
                    last = mm(b, hT[t][:, k, :], rwt[:, k, :], start=(k == 0), stop=(k == KD - 1))
                filled(("lg", t), last)

            project_out(0, 0, KD)
            project_out(1, 0, 2)
            turn_state(0)
            project_out(1, 2, 4)
            router(0)
            project_out(1, 4, KD)
            pe.wait_ge(S.mask_ready, 1)
            b, count_bank = fill("rank"), fill("cnt")
            mm(b[:, 0:E], tri, maskt[:, 0, :], start=True, stop=True)
            mm(b[:, E:2 * E], ones, maskt[:, 0, :], start=True, stop=False)
            mm(count_bank[:, 0:E], ones, maskt[:, 0, :], start=True, stop=False)
            turn_state(1)
            router(1)
            pe.wait_ge(S.mask_ready, 2)
            filled("rank", mm(b[:, E:2 * E], tri, maskt[:, 1, :], start=False, stop=True))
            filled("cnt", mm(count_bank[:, 0:E], ones, maskt[:, 1, :], start=False, stop=True))

            def free(bank):
                release, value = plan[turns[bank][-1]][2]
                pe.wait_ge(named[release], value)

            def down_biases():
                pe.wait_ge(S.gateT_ready, 1)
                pe.wait_ge(in_bias, 32)
                for bank in range(4):
                    free(bank)
                for t in range(2):
                    for c in range(2):
                        mm(total(t, c), gateT[0:E, t * P:(t + 1) * P], bdown[0:E, c * 512:(c + 1) * 512],
                           start=False, stop=False, skip_group_check=True)

            G, U, X, Y = (psum[:, bank, :] for bank in range(4, 8))

            def gather(n, i):
                pe.wait_ge(S.built, n + 1)
                if not isinstance(n, int) or n:
                    pe.wait_ge(S.sT_ready, n)
                for k in range(KD):
                    for t in range(2):
                        for part in range(3):
                            last = mm(X[:, k * SLOTS:(k + 1) * SLOTS], xn3[:, t, part, k * P:(k + 1) * P],
                                      ph[i][:, t, :], start=(t == 0 and part == 0), stop=(t == 1 and part == 2))
                last.then_inc(S.gathered, 1)

            def turn(n, i):
                pe.wait_ge(S.xe_ready, n + 1)
                for c in range(2):
                    for t in range(2):
                        j = 2 * c + t
                        last = nc.tensor.transpose(X[:, j * P:(j + 1) * P], wp[i][:, t, 64 - 64 * c:192 - 64 * c],
                                                   ident)
                last.then_inc(S.turned, 1)

            def biases(i, first):
                for half in range(2):
                    for o, b in ((0, G), (FF, U)):
                        last = mm(b[64 * half:64 * half + 64, :], pick[i],
                                  biasgu[:, o + half * 512:o + half * 512 + 512], start=first, stop=not first)
                return last

            def gate_up(n, i, loads, bias_last=False):
                if not bias_last:
                    biases(i, True)
                pe.wait_ge(S.xe_ready, n + 1)
                for k in range(KD):
                    pe.wait_ge(in_gu[i][k], loads)
                    for o, b in ((0, G), (FF, U)):
                        for half in range(2):
                            last = mm(b[64 * half:64 * half + 64, :], xe[i][:, k, :],
                                      gu[i][k][:, o + half * 512:o + half * 512 + 512],
                                      start=(k == 0 and bias_last), stop=(k == KD - 1 and not bias_last))
                    if k == KD - 1 and bias_last:
                        last = biases(i, False)
                    last.then_inc(S.gu_done, 1)

            def turn_act(n):
                pe.wait_ge(S.act_ready, n + 1)
                for c in range(4):
                    last = nc.tensor.transpose(Y[:, c * P:(c + 1) * P], a_s[:, c * P:(c + 1) * P], ident)
                last.then_inc(S.aT_done, 1)

            def down(n, loads):
                pe.wait_ge(S.aT_ready, n + 1)
                for i in range(4):
                    pe.wait_ge(in_dn[i], loads)
                    for u in range(2):
                        k = 2 * i + u
                        for c in range(2):
                            last = mm(Y[64 * c:64 * c + 64, :], aT[:, k % 4, 64 * (k // 4):64 * (k // 4) + 64],
                                      dn[i][:, u, c * 512:(c + 1) * 512], start=(k == 0), stop=(k == KD - 1))
                    last.then_inc(S.dn_done, 1)

            def scatter(n, i):
                pe.wait_ge(S.y_ready, n + 1)
                for t in range(2):
                    for c in range(2):
                        last = mm(total(t, c), sT[i][:, 2 * c + t, :], y_s, start=False, stop=False,
                                  skip_group_check=True)
                last.then_inc(S.scattered, 1)

            def item(n, i, gu_loads, dn_loads, final=False):
                gate_up(n, i, gu_loads)
                if not final:
                    gather(n + 1, 1 - i)
                scatter(n - 1, 1 - i)
                if not final:
                    turn(n + 1, 1 - i)
                turn_act(n)
                down(n, dn_loads)

            free(6)
            pe.wait_ge(S.split_ready, 2)
            gather(0, 0)
            pe.wait_ge(S.gate_ready, 2)
            b = fill("gt")
            for t in range(2):
                last = nc.tensor.transpose(b[0:E, t * P:(t + 1) * P], gate[:, t, :], ident)
            filled("gt", last)
            for bank in (4, 5, 7):
                free(bank)
            pe.wait_ge(in_bias, 32)
            gate_up(0, 0, 16, bias_last=True)
            turn(0, 0)
            down_biases()
            turn_act(0)
            down(0, 16)
            gather(1, 1)
            turn(1, 1)
            with pe.Fori(0, E // 2 - 1) as it:
                item(2 * it + 1, 1, 16 * it + 16, 32 * it + 32)
                item(2 * it + 2, 0, 16 * it + 32, 32 * it + 48)
            item(E - 1, 1, 16 * (E // 2), 16 * E, final=True)
            scatter(E - 1, 1)
            pe.wait_ge(S.overflow_ready, 1)
            count = pe.value_load(ovni[0:1, :], min_val=0, max_val=EXTRA)
            with pe.If(count > 0):
                with pe.Fori(0, count) as j:
                    n = j + E
                    gather(n, 0)
                    turn(n, 0)
                    gate_up(n, 0, 16 * j + 16 * (E // 2 + 1))
                    turn_act(n)
                    down(n, 16 * j + 16 * (E + 1))
                    scatter(n, 0)

        @block.scalar
        def _(act):
            f = nc.scalar.activation

            def full(job):
                bank, turn, _ = plan[job]
                act.wait_ge(bank_full[bank], turn + 1)
                return psum[:, bank, :]

            spare = [0]

            def load_table(func):
                f(tables[:, spare[0]:spare[0] + 1], warm, func)
                spare[0] += 1

            act.wait_ge(S.cols_clear, 1)
            load_table(ACT.Sqrt)
            for t in range(3):
                act.wait_ge(in_x[t], 32 if t == 0 else 16)
                r = TR[t]
                f(junk[0:r, :], xpos[0:r, t, :], ACT.Square, accum_out=ssx[0:r, t:t + 1]).then_inc(S.xss_ready, 1)
                act.wait_ge(S.xvar_ready, t + 1)
                f(rsx[:, t:t + 1], ssx[:, t:t + 1], ACT.Sqrt).then_inc(S.xroot_ready, 1)
            b = full("par")
            nc.scalar.copy(par, b[:, 0:R_END])
            nc.scalar.copy(dw, b[:, 128:128 + TAPS * CT]).then_inc(S.par_ready, 1)
            b = full("ckv")
            nc.scalar.copy(ckvn, b[:, 0:L])
            f(sqk, b[:, 0:L], ACT.Square).then_inc(S.squares, 1)
            nc.scalar.copy(kpeT[0:ROPE, :], full("kpe")[0:ROPE, 0:L]).then_inc(S.kpe_ready, 1)
            b = full("q").rearrange("p (j n) -> p j n", j=2)
            nc.scalar.copy(qnT, b)
            f(sqq, b, ACT.Square).then_inc(S.squares, 1)

            def conv_gate(j):
                if j >= 2:
                    act.wait_ge(S.convin_ready, j - 1)
                f(sig[:, j % 2, :], full(("cg", j))[:, 0:L], ACT.Sigmoid).then_inc(S.csig_ready, 1)

            conv_gate(0)
            act.wait_ge(S.lvar_ready, 1)
            f(rsb, rsb, ACT.Sqrt).then_inc(S.lroot_ready, 1)
            act.wait_ge(S.lvar_ready, 2)
            f(rsb2, rsb2, ACT.Sqrt).then_inc(S.lroot_ready, 1)
            conv_gate(1)
            act.wait_ge(S.pads_clear, 2)
            for t in range(3):
                for c in range(2):
                    b = full(("kvb", t, c))[0:TR[t], :].rearrange("p (h d) -> p h d", h=4)
                    kv_heads = kk[0:TR[t], t, :].rearrange("p (h d) -> p h d", h=H)[:, 4 * c:4 * c + 4, :]
                    v_heads = v[0:TR[t], t, :].rearrange("p (h d) -> p h d", h=H)[:, 4 * c:4 * c + 4, :]
                    nc.scalar.copy(kv_heads[:, :, 0:NOPE], b[:, :, 0:NOPE])
                    nc.scalar.copy(v_heads, b[:, :, NOPE:NOPE + VD]).then_inc(S.v_ready, 1)
            b = full("kpet")
            for t in range(3):
                kv_heads = kk[0:TR[t], t, :].rearrange("p (h d) -> p h d", h=H)
                last = nc.scalar.copy(kv_heads[:, :, NOPE:HD], b[0:TR[t], t * ROPE:(t + 1) * ROPE].unsqueeze(1)
                                      .to_broadcast([TR[t], H, ROPE]))
            last.then_inc(S.kraw_ready, 1)
            act.wait_ge(S.kraw_ready, 1)
            f(head_sq[0], kk.rearrange("p t c -> p (t c)"), ACT.Square).then_inc(S.ksq_ready, 1)
            conv_gate(2)
            act.wait_ge(S.khvar_ready, 1)
            f(hs, hs, ACT.Sqrt).then_inc(S.khroot_ready, 1)
            for t in range(2):
                for c in range(2):
                    nc.scalar.copy(q[:, t, c * 384:(c + 1) * 384], full(("qb", t, c))[:, 0:384]
                                   ).then_inc(S.qraw_ready, 1)
            act.wait_ge(S.qraw_ready, 4)
            f(head_sq[1], q.rearrange("p t c -> p (t c)"), ACT.Square).then_inc(S.qsq_ready, 1)
            conv_gate(3)
            act.wait_ge(in_cols, 64)
            for t in range(3):
                r = TR[t]
                for c in range(2 if t < 2 else 1):
                    n = 4 if t < 2 else 8
                    b = full(("kt", t, c))[0:HD, 0:n * r].rearrange("p (h j) -> p h j", h=n)
                    f(kT[0:HD, 4 * c:4 * c + n, t * P:t * P + r], b, ACT.Copy, scale=knc[0:HD, :]
                      ).then_inc(S.kT_ready, 1)
            act.wait_ge(S.qhvar_ready, 1)
            f(hsq, hsq, ACT.Sqrt).then_inc(S.qhroot_ready, 1)

            def heads_out(j):
                nc.scalar.copy(oT[:, j, :], full(("ot", j))[:, 0:SEQ]).then_inc(S.oT_ready, 1)

            def gate_out(s):
                f(gT[:, s, :], full(("gate", s))[:, 0:SEQ], ACT.Identity, bias=par[:, R_GB + s:R_GB + s + 1]
                  ).then_inc(S.gT_ready, 1)

            gate_out(0)
            for s in range(2 * H):
                h, t = s // 2, s % 2
                act.wait_ge(S.max_ready, s + 1)
                f(prob[:, t, 0:span(t)], sm[:, t, 0:span(t)], ACT.Exp, bias=nmx[:, t:t + 1],
                  scale=qscale[:, t * H + h:t * H + h + 1], accum_out=psm[:, t:t + 1]).then_inc(S.exp_ready, 1)
                if s + 1 < 2 * H:
                    gate_out(s + 1)
                if s and s % 4 == 0:
                    heads_out(s // 4 - 1)
                b = full(("pt", s))
                n = span(t) // P
                nc.scalar.copy(probT[:, t, 0:n * P], b[:, 0:n * P])
                nc.scalar.copy(probT[0:META, t, n * P:(n + 1) * P], b[0:META, n * P:(n + 1) * P]
                               ).then_inc(S.probT_ready, 1)
            heads_out(3)
            act.wait_ge(S.gT_ready, 2 * H)
            f(gT[:, 8:16, :], gT[:, 8:16, :], ACT.Sigmoid).then_inc(S.gates_ready, 1)
            act.wait_ge(S.lncent_ready, 1)
            f(sqc, acc, ACT.Square).then_inc(S.lnsq_ready, 1)
            f(gT[:, 0:8, :], gT[:, 0:8, :], ACT.Sigmoid).then_inc(S.gates_ready, 1)
            act.wait_ge(S.lnvar_ready, 1)
            f(rsb2, rsb2, ACT.Sqrt).then_inc(S.lnroot_ready, 1)
            act.wait_ge(S.lny_ready, 1)
            for j in range(CT):
                last = f(acc[:, j, :], acc[:, j, :], ACT.Silu, bias=par[:, R_LNB + j:R_LNB + j + 1],
                         scale=par[:, R_LNW + j:R_LNW + j + 1])
            last.then_inc(S.silu_ready, 1)
            for t in range(2):
                act.wait_ge(S.h1_ready, 2 * t + 2)
                f(xn[:, t, :], h1[:, t, :], ACT.Square, accum_out=ssh[:, t:t + 1]).then_inc(S.h1ss_ready, 1)
                act.wait_ge(S.h1var_ready, t + 1)
                f(rsh[:, t:t + 1], ssh[:, t:t + 1], ACT.Sqrt).then_inc(S.h1root_ready, 1)
                act.wait_ge(S.xn_ready, t + 1)
                nc.scalar.copy(xn3[:, t, 0, :], xn[:, t, :]).then_inc(S.hi_ready, 1)
                load_table(ACT.Exp)
                act.wait_ge(S.top_ready, t + 1)
                e4 = tk[:, 4 * t:4 * t + 4]
                f(e4, e4, ACT.Exp).then_inc(S.exp4_ready, 1)
                act.wait_ge(S.rest_ready, t + 1)
                nc.scalar.copy(xn3[:, t, 1, :], rest).then_inc(S.mid_ready, 1)
                if t == 0:
                    load_table(ACT.Sqrt)
            X, Y = psum[:, 6, :], psum[:, 7, :]

            def rows_out(n, i):
                act.wait_ge(S.gathered, n + 1)
                nc.scalar.copy(xe[i], X.rearrange("p (k s) -> p k s", k=KD)).then_inc(S.xe_ready, 1)

            def turned_out(n, i):
                act.wait_ge(S.turned, n + 1)
                nc.scalar.copy(sT[i], X.rearrange("p (j s) -> p j s", j=4)).then_inc(S.sT_ready, 1)

            def sigmoid(n):
                act.wait_ge(S.g_ready, n + 1)
                f(sg, g_s, ACT.Sigmoid, scale=ALPHA).then_inc(S.sg_ready, 1)

            def act_out(n):
                act.wait_ge(S.aT_done, n + 1)
                nc.scalar.copy(aT, Y.rearrange("p (c s) -> p c s", c=4)).then_inc(S.aT_ready, 1)

            def result_out(n):
                act.wait_ge(S.dn_done, 4 * n + 4)
                nc.scalar.copy(y_s, Y).then_inc(S.y_ready, 1)

            def item(n, i, final=False):
                if not final:
                    rows_out(n + 1, 1 - i)
                sigmoid(n)
                if not final:
                    turned_out(n + 1, 1 - i)
                act_out(n)
                result_out(n)

            rows_out(0, 0)
            nc.scalar.copy(gateT[0:E, :], full("gt")[0:E, 0:SEQ]).then_inc(S.gateT_ready, 1)
            turned_out(0, 0)
            sigmoid(0)
            act_out(0)
            result_out(0)
            rows_out(1, 1)
            turned_out(1, 1)
            with act.Fori(0, E // 2 - 1) as it:
                item(2 * it + 1, 1)
                item(2 * it + 2, 0)
            item(E - 1, 1, final=True)
            act.wait_ge(S.overflow_ready, 1)
            count = act.value_load(ovni[0:1, :], min_val=0, max_val=EXTRA)
            with act.If(count > 0):
                with act.Fori(0, count) as j:
                    n = j + E
                    rows_out(n, 0)
                    turned_out(n, 0)
                    sigmoid(n)
                    act_out(n)
                    result_out(n)
            act.wait_ge(S.scattered, count + E)
            for i in range(2):
                nc.scalar.copy(ysb[:, i, :], psum[:, i, :]).then_inc(S.fin_act, 1)

        @block.vector
        def _(dve):
            chain = [0]
            tt, ts, stt = nc.vector.tensor_tensor, nc.vector.tensor_scalar, nc.vector.scalar_tensor_tensor

            def link(ins):
                chain[0] += 1
                ins.then_inc(dve_step, 1)
                dve.wait_ge(dve_step, chain[0])

            def full(job):
                bank, turn, _ = plan[job]
                dve.wait_ge(bank_full[bank], turn + 1)
                return psum[:, bank, :]

            for t in range(3):
                dve.wait_ge(S.xss_ready, t + 1)
                ts(ssx[:, t:t + 1], ssx[:, t:t + 1], 1.0 / D, EPS, ALU.mult, ALU.add).then_inc(S.xvar_ready, 1)
                dve.wait_ge(S.xroot_ready, t + 1)
                link(nc.vector.reciprocal(rsx[:, t:t + 1], rsx[:, t:t + 1]))
                r = TR[t]
                ts(xpos[0:r, t, :], xpos[0:r, t, :], rsx[0:r, t:t + 1], None, ALU.mult).then_inc(S.xs_ready, 1)
            dve.wait_ge(S.par_ready, 1)
            for t in range(3):
                r = TR[t]
                for c in range(2 if t < 2 else 1):
                    n = 4 if t < 2 else 8
                    b = full(("hn", t, c))[:, 0:n * r].rearrange("p (k j) -> p k j", k=n)
                    w = par[:, R_ATTN + 4 * c:R_ATTN + 4 * c + n].unsqueeze(2).to_broadcast([P, n, r])
                    tt(hnT[:, 4 * c:4 * c + n, t * P:t * P + r], b, w, ALU.mult).then_inc(S.hn_ready, 1)

            def conv_in(j):
                b = full(("ca", j))
                dve.wait_ge(S.csig_ready, j + 1)
                tt(hc[:, j, PAD:], b[:, 0:L], sig[:, j % 2, :], ALU.mult).then_inc(S.convin_ready, 1)

            taps = [(j, k) for j in range(CT) for k in range(TAPS)]
            tap = iter(taps)

            def conv_taps(n):
                for _ in range(n):
                    j, k = next(tap, (None, None))
                    if j is None:
                        return
                    w = dw[:, k * CT + j:k * CT + j + 1]
                    if k == 0:
                        ins = ts(acc[:, j, :], hc[:, j, 0:SEQ], w, par[:, R_DWB + j:R_DWB + j + 1], ALU.mult, ALU.add)
                    else:
                        ins = stt(acc[:, j, :], hc[:, j, k:k + SEQ], w, acc[:, j, :], ALU.mult, ALU.add)
                    if (j, k) == taps[-1]:
                        ins.then_inc(S.conv_ready, 1)
                    else:
                        link(ins)

            dve.wait_ge(S.pads_clear, 1)
            conv_in(0)
            ts(rsb, full("ssk")[:, 0:L], 1.0 / KVL, EPS, ALU.mult, ALU.add).then_inc(S.lvar_ready, 1)
            ts(rsb2, full("ssq")[:, 0:SEQ], 1.0 / QL, EPS, ALU.mult, ALU.add).then_inc(S.lvar_ready, 1)
            dve.wait_ge(S.lroot_ready, 1)
            link(nc.vector.reciprocal(rsb, rsb))
            stt(ckvn, ckvn, par[:, R_KVA:R_KVA + 1], rsb, ALU.mult, ALU.mult).then_inc(S.lat_ready, 1)
            dve.wait_ge(S.lroot_ready, 2)
            link(nc.vector.reciprocal(rsb2, rsb2))
            for j in range(2):
                last = stt(qnT[:, j, :], qnT[:, j, :], par[:, R_QA + j:R_QA + j + 1], rsb2, ALU.mult, ALU.mult)
            last.then_inc(S.lat_ready, 1)
            conv_in(1)
            conv_taps(24)
            conv_in(2)
            dve.wait_ge(in_cols, 64)

            def rotary(y, tiles, nr, rope, sq_ready):
                n, half = tiles * H, ROPE // 2
                heads = y.rearrange("p t (h d) -> p (t h) d", d=HD)
                weighted = tmp[:, 0:n * ROPE]
                link(tt(weighted.rearrange("p (g d) -> p g d", d=ROPE), heads[:, :, NOPE:HD],
                        nr.unsqueeze(1).to_broadcast([P, n, ROPE]), ALU.mult))
                w4 = weighted.rearrange("p (t h d) -> p t h d", t=tiles, h=H)
                y4 = y.rearrange("p t (h d) -> p t h d", d=HD)
                angles = const[:, rope:rope + ROPE * tiles].rearrange("p (t c) -> p t c", t=tiles)
                cos = angles[:, :, 0:half].unsqueeze(2).to_broadcast([P, tiles, H, half])
                sin = angles[:, :, half:ROPE].unsqueeze(2).to_broadcast([P, tiles, H, half])
                part = [tmp[:, (2 + i) * n * half:(3 + i) * n * half].rearrange("p (t h d) -> p t h d", t=tiles, h=H)
                        for i in range(4)]
                tt(part[0], w4[:, :, :, 0:half], cos, ALU.mult)
                tt(part[1], w4[:, :, :, half:ROPE], sin, ALU.mult)
                tt(part[2], w4[:, :, :, half:ROPE], cos, ALU.mult)
                link(tt(part[3], w4[:, :, :, 0:half], sin, ALU.mult))
                dve.wait_ge(sq_ready, 1)
                tt(y4[:, :, :, NOPE:NOPE + half], part[0], part[1], ALU.subtract)
                return tt(y4[:, :, :, NOPE + half:HD], part[2], part[3], ALU.add)

            def head_variance(ss, sq, ready):
                link(nc.vector.tensor_reduce(ss, sq.rearrange("p (g d) -> p g d", d=HD), AX_X, ALU.add))
                ts(ss, ss, 1.0 / HD, EPS, ALU.mult, ALU.add).then_inc(ready, 1)

            dve.wait_ge(S.kraw_ready, 1)
            link(rotary(kk, 3, knr, C_RK, S.ksq_ready))
            head_variance(hs, head_sq[0], S.khvar_ready)
            conv_taps(1)
            dve.wait_ge(S.khroot_ready, 1)
            link(nc.vector.reciprocal(hs, hs))
            k_heads = kk.rearrange("p t (h d) -> p (t h) d", d=HD)
            tt(k_heads, k_heads, hs.unsqueeze(2).to_broadcast([P, 3 * H, HD]), ALU.mult).then_inc(S.k_ready, 1)
            dve.wait_ge(S.qraw_ready, 4)
            rotary(q, 2, qnr, C_RQ, S.qsq_ready).then_inc(S.q_ready, 1)
            conv_in(3)
            head_variance(hsq, head_sq[1], S.qhvar_ready)
            for t in range(2):
                for c in range(2):
                    ts(qT[0:HD, 4 * c:4 * c + 4, t * P:(t + 1) * P],
                       full(("qt", t, c))[0:HD, :].rearrange("p (h j) -> p h j", h=4), qnc[0:HD, :], None,
                       ALU.mult).then_inc(S.qT_ready, 1)
            dve.wait_ge(S.qhroot_ready, 1)
            link(nc.vector.reciprocal(hsq, hsq))
            ts(qscale, hsq, SCALE, None, ALU.mult)
            link(ts(qnscale, hsq, -SCALE, None, ALU.mult))
            for s in range(2 * H):
                h, t = s // 2, s % 2
                b = full(("s", s))
                first = C_MASK + (P if t == 0 else 0)
                link(nc.vector.tensor_tensor_reduce(sm[:, t, 0:span(t)], b[:, 0:span(t)],
                                                    const[:, first:first + span(t)], 1.0, 4 * NEG, ALU.add, ALU.max,
                                                    mx[:, t:t + 1]))
                ts(nmx[:, t:t + 1], mx[:, t:t + 1], qnscale[:, t * H + h:t * H + h + 1], None, ALU.mult
                   ).then_inc(S.max_ready, 1)
                conv_taps(2)
                dve.wait_ge(S.exp_ready, s + 1)
                link(nc.vector.reciprocal(prs[:, t:t + 1], psm[:, t:t + 1]))
                ts(prob[:, t, 0:span(t)], prob[:, t, 0:span(t)], prs[:, t:t + 1], None, ALU.mult
                   ).then_inc(S.prob_ready, 1)
                conv_taps(4)
            conv_taps(len(taps))
            mean_sum = full("lnmu")[:, 0:SEQ].unsqueeze(1).to_broadcast([P, CT, SEQ])
            dve.wait_ge(S.conv_ready, 1)
            stt(acc, mean_sum, -1.0 / CONV, acc, ALU.mult, ALU.add).then_inc(S.lncent_ready, 1)

            def attention_mix(j):
                b = full(("ym", j)).rearrange("p (i n) -> p i n", i=2)
                dve.wait_ge(S.gates_ready, 1)
                tt(mixT[:, 2 * j:2 * j + 2, :], b, gT[:, 8 + 2 * j:10 + 2 * j, :], ALU.mult
                   ).then_inc(S.ymix_ready, 1)

            attention_mix(0)
            attention_mix(1)
            ts(rsb2, full("lnvar")[:, 0:SEQ], 1.0 / CONV, EPS, ALU.mult, ALU.add).then_inc(S.lnvar_ready, 1)
            dve.wait_ge(S.lnroot_ready, 1)
            link(nc.vector.reciprocal(rsb2, rsb2))
            tt(acc, acc, rsb2.unsqueeze(1).to_broadcast([P, CT, SEQ]), ALU.mult).then_inc(S.lny_ready, 1)
            attention_mix(2)
            attention_mix(3)
            dve.wait_ge(S.ymix_ready, 4)
            dve.wait_ge(S.gates_ready, 2)
            for j in range(4):
                b = full(("yc", j)).rearrange("p (i n) -> p i n", i=2)
                if j:
                    dve.wait_ge(S.mix_ready, j)
                link(tt(half_mix, b, gT[:, 2 * j:2 * j + 2, :], ALU.mult))
                tt(mixT[:, 2 * j:2 * j + 2, :], mixT[:, 2 * j:2 * j + 2, :], half_mix, ALU.add
                   ).then_inc(S.mix_ready, 1)
            dve.wait_ge(in_router, 48)
            tt(rwt, rwt, par[:, R_FFN:R_FFN + KD].unsqueeze(2).to_broadcast([P, KD, E]), ALU.mult
               ).then_inc(S.router_ready, 1)
            logits = tk[:, 8:72].rearrange("p (t e) -> p t e", t=2)
            v8 = tk[:, 72:88].rearrange("p (t e) -> p t e", t=2)
            i8 = tk[:, 88:104].bitcast(U32).rearrange("p (t e) -> p t e", t=2)
            f8 = tk[:, 104:120].rearrange("p (t e) -> p t e", t=2)
            e4 = tk[:, 0:8].rearrange("p (t e) -> p t e", t=2)
            sum4, inv4 = tk[:, 120:122], tk[:, 122:124]
            hot = tk[:, 128:384].rearrange("p (t k e) -> p t k e", t=2, k=TOPK)

            def low_part(t):
                dve.wait_ge(S.mid_ready, t + 1)
                tt(xn3[:, t, 2, :], rest, xn3[:, t, 1, :], ALU.subtract).then_inc(S.split_ready, 1)

            for t in range(2):
                for c in range(2):
                    nc.vector.tensor_copy(h1[:, t, c * 512:(c + 1) * 512], full(("ho", t, c))
                                          ).then_inc(S.h1_ready, 1)
                for c in range(2):
                    nc.vector.tensor_copy(hT[t][:, 4 * c:4 * c + 4, :],
                                          full(("ht", t, c)).rearrange("p (k n) -> p k n", k=4)
                                          ).then_inc(S.hT_ready, 1)
                dve.wait_ge(S.h1ss_ready, t + 1)
                ts(ssh[:, t:t + 1], ssh[:, t:t + 1], 1.0 / D, EPS, ALU.mult, ALU.add).then_inc(S.h1var_ready, 1)
                dve.wait_ge(S.h1root_ready, t + 1)
                link(nc.vector.reciprocal(rsh[:, t:t + 1], rsh[:, t:t + 1]))
                stt(xn[:, t, :], h1[:, t, :], rsh[:, t:t + 1], fnw, ALU.mult, ALU.mult).then_inc(S.xn_ready, 1)
                link(stt(logits[:, t, :], full(("lg", t))[:, 0:E], rsh[:, t:t + 1], router_bias, ALU.mult, ALU.add))
                nc.vector.max(v8[:, t, :], logits[:, t, :]).then_inc(S.logits_ready, 1)
                dve.wait_ge(S.logits_ready, t + 1)
                tt(e4[:, t, :], v8[:, t, 0:TOPK], v8[:, t, 0:1].to_broadcast([P, TOPK]), ALU.subtract
                   ).then_inc(S.top_ready, 1)
                link(nc.vector.max_index(i8[:, t, :], v8[:, t, :], logits[:, t, :]))
                link(nc.vector.tensor_copy(f8[:, t, :], i8[:, t, :]))
                link(tt(hot[:, t], iota[:, 0:E].unsqueeze(1).to_broadcast([P, TOPK, E]),
                        f8[:, t, 0:TOPK].unsqueeze(2).to_broadcast([P, TOPK, E]), ALU.is_equal))
                nc.vector.tensor_reduce(maskt[:, t, :], hot[:, t].rearrange("p k e -> p e k"), AX_X, ALU.add
                                        ).then_inc(S.mask_ready, 1)
                dve.wait_ge(S.hi_ready, t + 1)
                tt(rest, xn[:, t, :], xn3[:, t, 0, :], ALU.subtract).then_inc(S.rest_ready, 1)
                dve.wait_ge(S.exp4_ready, t + 1)
                link(nc.vector.tensor_reduce(sum4[:, t:t + 1], e4[:, t, :], AX_X, ALU.add))
                link(nc.vector.reciprocal(inv4[:, t:t + 1], sum4[:, t:t + 1]))
                link(ts(e4[:, t, :], e4[:, t, :], inv4[:, t:t + 1], None, ALU.mult))
                dve.wait_ge(S.mask_ready, t + 1)
                link(tt(hot[:, t], hot[:, t], e4[:, t, :].unsqueeze(2).to_broadcast([P, TOPK, E]), ALU.mult))
                nc.vector.tensor_reduce(gate[:, t, :], hot[:, t].rearrange("p k e -> p e k"), AX_X, ALU.add
                                        ).then_inc(S.gate_ready, 1)
                if t == 0:
                    low_part(t)
            link(stt(rankp, full("rank")[:, 0:2 * E].rearrange("p (t e) -> p t e", t=2), 1.0, maskt, ALU.add,
                     ALU.mult))
            ts(rankp, rankp, -1.0, None, ALU.add).then_inc(S.rank_ready, 1)
            dve.wait_ge(S.rank_ready, 1)
            dve.wait_ge(S.gate_ready, 2)

            G, U = psum[:, 4, :], psum[:, 5, :]

            def build(e, i, base):
                numbers = iota[:, 0:SLOTS] if isinstance(base, int) else iota[:, bass.ds(base, SLOTS)]
                col = slice(e, e + 1) if isinstance(e, int) else bass.ds(e, 1)
                for t in range(2):
                    ts(ph[i][:, t, :], numbers, rankp[:, t, col], None, ALU.is_equal)
                    ts(wp[i][:, t, SLOTS:2 * SLOTS], numbers, rankp[:, t, col], gate[:, t, col], ALU.is_equal,
                       ALU.mult)
                nc.vector.tensor_copy(pick[i], ident[:, col].to_broadcast([P, SLOTS])).then_inc(S.built, 1)

            def activations(n):
                dve.wait_ge(S.gu_done, 8 * n + 8)
                ts(g_s, G, LIMIT, None, ALU.min).then_inc(S.g_ready, 1)
                ts(a_s, U, LIMIT, -LIMIT, ALU.min, ALU.max).then_inc(S.a_step, 1)
                dve.wait_ge(S.g_ready, n + 1)
                dve.wait_ge(S.a_step, 2 * n + 1)
                stt(a_s, a_s, 1.0, g_s, ALU.add, ALU.mult).then_inc(S.a_step, 1)
                dve.wait_ge(S.a_step, 2 * n + 2)
                dve.wait_ge(S.sg_ready, n + 1)
                tt(a_s, a_s, sg, ALU.mult).then_inc(S.act_ready, 1)

            dve.wait_ge(S.pick_clear, 2)
            build(0, 0, 0)
            low_part(1)
            counts = ov_s[:, 0:E]
            nc.vector.tensor_copy(counts, full("cnt")[:, 0:E]).then_inc(S.cnt_ready, 1)
            build(1, 1, 0)
            valid, place = ov_s[:, 32:128], ov_s[:, 128:224]
            code = ov_s[:, 224:320]
            dve.wait_ge(S.cnt_ready, 1)
            for b in range(3):
                last = ts(valid[:, 32 * b:32 * b + 32], counts, float(SLOTS * (b + 1)), None, ALU.is_gt)
            link(last)
            nc.vector.tensor_tensor_scan(place, ones[:, 0:96], valid, 0.0, ALU.mult, ALU.add)
            tt(code, valid, iota[:, 0:96], ALU.mult)
            link(nc.vector.tensor_reduce(ovn, valid, AX_X, ALU.add))
            for j in range(EXTRA):
                link(stt(valid, place, float(j + 1), code, ALU.is_equal, ALU.mult, accum_out=ovf[:, j:j + 1]))
            turns1, turns2 = ov_s[:, 32:48], ov_s[:, 48:64]
            ts(turns1, ovf, 32.0, None, ALU.is_ge)
            link(ts(turns2, ovf, 64.0, None, ALU.is_ge))
            link(tt(turns1, turns1, turns2, ALU.add))
            link(ts(turns2, turns1, float(SLOTS), float(SLOTS), ALU.mult, ALU.add))
            link(stt(ovf, turns1, -32.0, ovf, ALU.mult, ALU.add))
            nc.vector.tensor_copy(ove, ovf)
            nc.vector.tensor_copy(ovb, turns2)
            nc.vector.tensor_copy(ovni, ovn).then_inc(S.overflow_ready, 1)
            activations(0)
            with dve.Fori(0, E // 2 - 1) as it:
                build(2 * it + 2, 0, 0)
                activations(2 * it + 1)
                build(2 * it + 3, 1, 0)
                activations(2 * it + 2)
            activations(E - 1)
            dve.wait_ge(S.overflow_ready, 1)
            count = dve.value_load(ovni[0:1, :], min_val=0, max_val=EXTRA)
            with dve.If(count > 0):
                with dve.Fori(0, count) as j:
                    e = dve.value_load(ove[0:1, bass.ds(j, 1)], min_val=0, max_val=E - 1)
                    base = dve.value_load(ovb[0:1, bass.ds(j, 1)], min_val=0, max_val=256 - SLOTS)
                    build(e, 0, base)
                    activations(j + E)
            dve.wait_ge(S.scattered, count + E)
            for i in range(2):
                nc.vector.tensor_copy(ysb[:, 2 + i, :], psum[:, 2 + i, :]).then_inc(S.fin_dve, 1)


_INS = ["x", "meta_tokens", "attn_norm_w", "w_in", "conv_dw_w", "conv_dw_b", "conv_ln_w", "conv_ln_b", "conv_pw2_w",
        "q_a_norm_w", "w_q_b", "kv_a_norm_w", "w_kv_b", "q_norm_w", "k_norm_w", "w_o_mla", "gate_b", "w_out",
        "ffn_norm_w", "router_w", "router_b", "w_gate_up", "b_gate_up", "w_down", "b_down"]


def kernel(**inputs):
    import concourse.bacc as bacc
    from concourse.bass_utils import run_bass_kernel_spmd

    nc = bacc.Bacc("TRN2", target_bir_lowering=False, num_devices=1)
    arrays = {f"in_{name}": np.ascontiguousarray(inputs[name]) for name in _INS}
    arrays["in_const"] = constants()
    args = {name[3:]: nc.dram_tensor(name, v.shape, mybir.dt.from_np(v.dtype), kind="ExternalInput").ap()
            for name, v in arrays.items()}
    out = nc.dram_tensor("out_y", (1, SEQ, D), F32, kind="ExternalOutput").ap()
    layer(nc, args, out)
    r = run_bass_kernel_spmd(nc, [arrays], core_ids=[0])
    return r.results[0]["out_y"]
```
